# Optimizing a Trainium2 kernel written in Bass

```python
import jax
import jax.numpy as jnp
from jax import lax
import numpy as np

D_MODEL = 1024
BATCH = 1
SEQ = 256
DEPTH = 2

HEAD_DIM = 64
H_A = 4
H_B = 4
H_C = 8
D_MIX = (H_A + H_B + H_C) * HEAD_DIM
IDX_HEADS = 8
IDX_DIM = 64
TOPK_MAX = 256
DILATIONS = ((128, 1), (512, 4), (2048, 16))
Q_BLOCK = 128
D_FF = 2816
N_MOD = 9
IN_COLS = 3 * D_MIX + IDX_HEADS * IDX_DIM + IDX_DIM + IDX_HEADS
EPS = 1e-6

kernel_name = 'hybrid_dsa_stickbreak_dilated_macaron_adaln'

def rms_norm(x, gain):
    xf = x.astype(jnp.float32)
    y = xf * lax.rsqrt(jnp.mean(xf * xf, axis=-1, keepdims=True) + EPS)
    return (y * gain.astype(jnp.float32)).astype(x.dtype)

def modulate(h, shift, scale):
    return h * (1 + scale) + shift

def swiglu(h, w_gate, w_up, w_down):
    g = jnp.einsum('bsd,df->bsf', h, w_gate)
    u = jnp.einsum('bsd,df->bsf', h, w_up)
    return jnp.einsum('bsf,fd->bsd', jax.nn.silu(g) * u, w_down)

def alibi_slopes():
    n = H_A + H_C
    slopes = jnp.exp2(-8.0 * jnp.arange(1, n + 1, dtype=jnp.float32) / n)
    idx = np.arange(n)
    return slopes[idx[idx % 3 == 2]], slopes[idx[idx % 3 != 2]]

def to_blocks(a):
    b, s = a.shape[0], a.shape[1]
    return jnp.moveaxis(a.reshape(b, s // Q_BLOCK, Q_BLOCK, *a.shape[2:]), 1, 0)

def from_blocks(a):
    nb, b = a.shape[0], a.shape[1]
    return jnp.moveaxis(a, 0, 1).reshape(b, nb * Q_BLOCK, *a.shape[3:])

def dsa_attention(q, k, v, qi, ki, wi, slopes, topk):
    s_len = q.shape[1]
    kpos = jnp.arange(s_len)
    scale = HEAD_DIM ** -0.5
    idx_scale = (IDX_DIM ** -0.5) * (IDX_HEADS ** -0.5)

    def block(args):
        qb, qib, wib, t0 = args
        tpos = t0 + jnp.arange(Q_BLOCK)
        rel = jnp.einsum('bthe,bse->bhts', qib, ki).astype(jnp.float32)
        score = jnp.einsum('bth,bhts->bts', wib.astype(jnp.float32), jax.nn.relu(rel)) * idx_scale
        score = jnp.where(kpos[None, None, :] <= tpos[None, :, None], score, -jnp.inf)
        _, sel = lax.top_k(score, topk)
        kg = jax.vmap(lambda kk, ii: kk[ii])(k, sel)
        vg = jax.vmap(lambda vv, ii: vv[ii])(v, sel)
        dist = tpos[None, :, None] - sel
        logits = jnp.einsum('bthd,btkhd->bhtk', qb, kg).astype(jnp.float32) * scale
        logits = logits - slopes[None, :, None, None] * dist[:, None].astype(jnp.float32)
        logits = jnp.where((dist >= 0)[:, None], logits, -jnp.inf)
        p = jax.nn.softmax(logits, axis=-1).astype(v.dtype)
        return jnp.einsum('bhtk,btkhd->bthd', p, vg)

    nb = s_len // Q_BLOCK
    out = lax.map(block, (to_blocks(q), to_blocks(qi), to_blocks(wi), jnp.arange(nb) * Q_BLOCK))
    return from_blocks(out)

def stick_breaking_attention(q, k, v):
    s_len = q.shape[1]
    kpos = jnp.arange(s_len)
    scale = HEAD_DIM ** -0.5

    def block(args):
        qb, t0 = args
        tpos = t0 + jnp.arange(Q_BLOCK)
        z = jnp.einsum('bthd,bshd->bhts', qb, k).astype(jnp.float32) * scale
        strict = kpos[None, :] < tpos[:, None]
        log_1m = jnp.where(strict, jax.nn.log_sigmoid(-z), 0.0)
        log_stay = lax.cumsum(log_1m, axis=3, reverse=True) - log_1m
        a = jnp.where(strict, jnp.exp(jax.nn.log_sigmoid(z) + log_stay), 0.0)
        return jnp.einsum('bhts,bshd->bthd', a.astype(v.dtype), v)

    nb = s_len // Q_BLOCK
    out = lax.map(block, (to_blocks(q), jnp.arange(nb) * Q_BLOCK))
    return from_blocks(out)

def dilated_attention(q, k, v, slopes):
    s_len = q.shape[1]
    scale = HEAD_DIM ** -0.5

    def block(args):
        qb, t0 = args
        tpos = t0 + jnp.arange(Q_BLOCK)
        lses, outs = [], []
        for window, dil in DILATIONS:
            dist = jnp.arange(window // dil + 1) * dil
            kidx = tpos[:, None] - dist[None, :]
            valid = kidx >= 0
            kidx = jnp.maximum(kidx, 0)
            kg = k[:, kidx]
            vg = v[:, kidx]
            logits = jnp.einsum('bthd,btnhd->bhtn', qb, kg).astype(jnp.float32) * scale
            logits = logits - slopes[:, None, None] * dist.astype(jnp.float32)[None, None, :]
            logits = jnp.where(valid[None, None], logits, -jnp.inf)
            m = jnp.max(logits, axis=-1, keepdims=True)
            p = jnp.exp(logits - m)
            l = jnp.sum(p, axis=-1, keepdims=True)
            outs.append(jnp.einsum('bhtn,btnhd->bthd', (p / l).astype(v.dtype), vg))
            lses.append(m + jnp.log(l))
        w = jax.nn.softmax(jnp.stack(lses, axis=0), axis=0)
        w = jnp.transpose(w, (0, 1, 3, 2, 4)).astype(v.dtype)
        return sum(w[i] * outs[i] for i in range(len(DILATIONS)))

    nb = s_len // Q_BLOCK
    out = lax.map(block, (to_blocks(q), jnp.arange(nb) * Q_BLOCK))
    return from_blocks(out)

def token_mixing(h, w_in, qn_a, kn_a, qn_c, kn_c, g_out, w_out, slopes_a, slopes_c):
    b, s_len, _ = h.shape
    topk = min(TOPK_MAX, s_len // 4)
    proj = jnp.einsum('bsd,de->bse', h, w_in)
    sizes = [H_A * HEAD_DIM] * 3 + [IDX_HEADS * IDX_DIM, IDX_DIM, IDX_HEADS] + [H_B * HEAD_DIM] * 3 + [H_C * HEAD_DIM] * 3
    offsets = np.cumsum(sizes)[:-1].tolist()
    qa, ka, va, qi, ki, wi, qb, kb, vb, qc, kc, vc = jnp.split(proj, offsets, axis=-1)
    heads = lambda t, n: t.reshape(b, s_len, n, HEAD_DIM)
    o_a = dsa_attention(rms_norm(heads(qa, H_A), qn_a), rms_norm(heads(ka, H_A), kn_a), heads(va, H_A),
                        qi.reshape(b, s_len, IDX_HEADS, IDX_DIM), ki, wi, slopes_a, topk)
    o_b = stick_breaking_attention(heads(qb, H_B), heads(kb, H_B), heads(vb, H_B))
    o_c = dilated_attention(rms_norm(heads(qc, H_C), qn_c), rms_norm(heads(kc, H_C), kn_c), heads(vc, H_C), slopes_c)
    wa, wb = H_A * HEAD_DIM, H_B * HEAD_DIM
    g_a, g_b, g_c = jnp.split(g_out, [wa, wa + wb])
    y = jnp.concatenate([rms_norm(o_a.reshape(b, s_len, -1), g_a),
                         rms_norm(o_b.reshape(b, s_len, -1), g_b),
                         rms_norm(o_c.reshape(b, s_len, -1), g_c)], axis=-1)
    return jnp.einsum('bse,ed->bsd', y, w_out)

def setup_inputs(seed: int = 0) -> dict:
    key = jax.random.key(seed)
    ks = jax.random.split(key, 24)
    f32 = jnp.float32
    L, D = DEPTH, D_MODEL

    def nrm(k, shape, scale):
        return jax.random.normal(k, shape, f32) * scale

    def gain(k, shape):
        return 1.0 + 0.05 * jax.random.normal(k, shape, f32)

    return {
        'x': nrm(ks[0], (BATCH, SEQ, D), 1.0),
        'c': nrm(ks[1], (BATCH, D), 1.0),
        'w_ada': nrm(ks[2], (L, D, N_MOD * D), 0.5 * D ** -0.5),
        'b_ada': nrm(ks[3], (L, N_MOD * D), 0.02),
        'norm_ffn1': gain(ks[4], (L, D)),
        'w_gate1': nrm(ks[5], (L, D, D_FF), D ** -0.5),
        'w_up1': nrm(ks[6], (L, D, D_FF), D ** -0.5),
        'w_down1': nrm(ks[7], (L, D_FF, D), D_FF ** -0.5),
        'norm_mix': gain(ks[8], (L, D)),
        'w_in': nrm(ks[9], (L, D, IN_COLS), D ** -0.5),
        'qn_a': gain(ks[10], (L, HEAD_DIM)),
        'kn_a': gain(ks[11], (L, HEAD_DIM)),
        'qn_c': gain(ks[12], (L, HEAD_DIM)),
        'kn_c': gain(ks[13], (L, HEAD_DIM)),
        'g_out': gain(ks[14], (L, D_MIX)),
        'w_out': nrm(ks[15], (L, D_MIX, D), D_MIX ** -0.5),
        'norm_ffn2': gain(ks[16], (L, D)),
        'w_gate2': nrm(ks[17], (L, D, D_FF), D ** -0.5),
        'w_up2': nrm(ks[18], (L, D, D_FF), D ** -0.5),
        'w_down2': nrm(ks[19], (L, D_FF, D), D_FF ** -0.5),
    }

def reference(x, c, w_ada, b_ada, norm_ffn1, w_gate1, w_up1, w_down1, norm_mix, w_in, qn_a, kn_a, qn_c, kn_c,
              g_out, w_out, norm_ffn2, w_gate2, w_up2, w_down2):
    slopes_a, slopes_c = alibi_slopes()
    cond = jax.nn.silu(c)
    for l in range(DEPTH):
        mod = jnp.einsum('bd,de->be', cond, w_ada[l]) + b_ada[l]
        sh1, sc1, g1, sh2, sc2, g2, sh3, sc3, g3 = [m[:, None, :] for m in jnp.split(mod, N_MOD, axis=-1)]
        h = modulate(rms_norm(x, norm_ffn1[l]), sh1, sc1)
        x = x + 0.5 * g1 * swiglu(h, w_gate1[l], w_up1[l], w_down1[l])
        h = modulate(rms_norm(x, norm_mix[l]), sh2, sc2)
        x = x + g2 * token_mixing(h, w_in[l], qn_a[l], kn_a[l], qn_c[l], kn_c[l], g_out[l], w_out[l], slopes_a, slopes_c)
        h = modulate(rms_norm(x, norm_ffn2[l]), sh3, sc3)
        x = x + 0.5 * g3 * swiglu(h, w_gate2[l], w_up2[l], w_down2[l])
    return x


_drawn_inputs = setup_inputs


def setup_inputs(seed=0):
    import zlib

    import numpy as np

    out = dict(_drawn_inputs(seed))
    spreads = {}
    factors = {'norm_ffn1': 3.479,
     'qn_a': 6.543,
     'kn_a': 7.548,
     'qn_c': 5.5,
     'kn_c': 6.939,
     'norm_ffn2': 4.286}
    for name, (base, spread) in spreads.items():
        noise = np.random.default_rng([zlib.crc32(name.encode()), seed]).standard_normal(out[name].shape)
        drawn = base * np.exp(spread * noise) if base else spread * noise
        out[name] = jnp.asarray(drawn.astype(out[name].dtype))
    for name, factor in factors.items():
        out[name] = (out[name] * factor).astype(out[name].dtype)
    return out
```

```python
from contextlib import ExitStack

import numpy as np

import concourse.bass as bass
from concourse import mybir

F32 = mybir.dt.float32
F32R = mybir.dt.float32r
BF16 = mybir.dt.bfloat16
I32 = mybir.dt.int32
ALU = mybir.AluOpType
ACT = mybir.ActivationFunctionType
AX_X = mybir.AxisListType.X

P = 128
HD = 64
H_A, H_B, H_C, H_I = 4, 4, 8, 8
DILATIONS = ((128, 1), (512, 4), (2048, 16))
EPS = 1e-6
NEG = -1e30
TAKEN = -3e38
CW = 256
NSLOT = 3
N_MOD = 9
GRP = 4


def slopes():
    n = H_A + H_C
    every = np.exp2(np.float32(-8.0) * np.arange(1, n + 1, dtype=np.float32) / np.float32(n))
    return [float(s) for i, s in enumerate(every) if i % 3 == 2], [float(s) for i, s in enumerate(every) if i % 3 != 2]


def build(nc, x, c, w_ada, b_ada, norm_ffn1, w_gate1, w_up1, w_down1, norm_mix, w_in, qn_a, kn_a, qn_c, kn_c,
          g_out, w_out, norm_ffn2, w_gate2, w_up2, w_down2, out):
    _, S, D = x.shape
    L = w_in.shape[0]
    FF = w_gate1.shape[2]
    KT = D // P
    TT = S // P
    NF = FF // CW
    FT = FF // P
    HALF = 512
    TOPK = min(256, S // 4)
    assert D == 1024 and S == 256 and FF % CW == 0 and TT == 2 and TOPK % 8 == 0

    sizes = [H_A * HD] * 3 + [H_I * HD, HD, H_I] + [H_B * HD] * 3 + [H_C * HD] * 3
    at = dict(zip(("qa", "ka", "va", "qi", "ki", "wi", "qb", "kb", "vb", "qc", "kc", "vc"), np.cumsum([0] + sizes[:-1]).tolist()))
    CHUNKS = [("qi", 0), ("qi", 1), ("ki", 0), ("ka", 0), ("qa", 0), ("va", 0), ("kb", 0), ("qb", 0), ("vb", 0),
              ("kc", 0), ("kc", 1), ("qc", 0), ("qc", 1), ("vc", 0), ("vc", 1)]
    NC = len(CHUNKS)
    NORMED = [n for n, (k, _) in enumerate(CHUNKS) if k in ("ka", "qa", "kc", "qc")]
    GAIN = {"qa": 0, "ka": 1, "qc": 2, "kc": 3}
    OUT_CHUNKS = [(0, 1), (1, 1), (2, 1), (3, 1), (4, 2), (6, 2)]
    U_FFN = (0, NF + NC // NSLOT + len(OUT_CHUNKS) // NSLOT)
    U_IN = NF
    U_OUT = NF + NC // NSLOT
    U_LAYER = U_FFN[1] + NF
    ADA_L = N_MOD * D // CW
    AHEAD = 2 * D // CW
    MID = ADA_L - 3 * NF
    CT = CW // P
    assert MID == 3 and KT * N_MOD == ADA_L * CT
    ADA_PRE = AHEAD // 2
    ADA_TURNS = (NF + 2 + NF, NF + 1)

    wide = lambda w: w.rearrange("l (k p) n -> p (l k) n", p=P)
    v_gate, v_up, v_down = map(wide, (w_gate1, w_up1, w_down1))
    v_gate2, v_up2, v_down2 = map(wide, (w_gate2, w_up2, w_down2))
    v_in, v_out, v_ada = map(wide, (w_in, w_out, w_ada))
    x_v = x.rearrange("b (t p) d -> p (b t) d", p=P)
    out_v = out.rearrange("b (t p) d -> p (b t) d", p=P)

    ctx = ExitStack()
    with ctx:
        def sb(name, shape, dt=F32):
            return ctx.enter_context(nc.sbuf_tensor(name, shape, dt))

        def sem(name):
            return ctx.enter_context(nc.semaphore(name))

        raw = [sb(f"raw{k}", [P, 8 * CW]) for k in range(NSLOT)]
        whi = [sb(f"whi{k}", [P, 8 * CW], F32R) for k in range(NSLOT)]
        wlo = [sb(f"wlo{k}", [P, 8 * CW], F32R) for k in range(NSLOT)]
        ada = sb("ada", [P, 2, KT, CW])
        xs = sb("xs", [P, TT, D])
        xn = sb("xn", [P, TT, D])
        hTf = sb("hTf", [P, KT, S])
        hhi = sb("hhi", [P, KT, S], F32R)
        hlo = sb("hlo", [P, KT, S], F32R)
        gate = sb("gate", [P, D])
        qk1 = sb("qk1", [P, 4, S])
        qk2 = sb("qk2", [P, 4, S])
        qbT = sb("qbT", [P, 2, S])
        kbT = sb("kbT", [P, 2, S])
        kiT = sb("kiT", [P, S])
        vs = sb("vs", [P, TT, D])
        wi = sb("wi", [P, TT, H_I])
        aliA = sb("aliA", [P, H_A, S])
        aliC = sb("aliC", [P, H_C, S])
        mult = sb("mult", [P, S], BF16)
        causal = sb("causal", [P, S])
        strictT = sb("strictT", [P, S], BF16)
        ident = sb("ident", [P, P])
        ones = sb("ones", [P, P])
        heads1 = sb("heads1", [P, P])
        upper = sb("upper", [P, P])
        zero16 = sb("zero16", [P, HALF], BF16)
        LG = [sb(f"LG{k}", [P, 4 * S]) for k in range(2)]
        pT = sb("pT", [P, TT, GRP, P])
        eb = sb("eb", [P, GRP * (S + P)])
        guhi = sb("guhi", [P, 2 * S], F32R)
        gulo = sb("gulo", [P, 2 * S], F32R)
        top8 = sb("top8", [P, 8])
        cT = sb("cT", [P, KT])
        acc = sb("acc", [P, 2, CW])
        modc = sb("modc", [P, (N_MOD + 2) * KT])
        biasL = sb("biasL", [P, N_MOD, KT])
        cols = sb("cols", [P, L, KT, 13])
        colL = sb("colL", [P, KT, 13])
        qkg = sb("qkg", [P, L, 4])
        qkgL = sb("qkgL", [P, 4])
        modA = sb("modA", [P, KT])
        modB = sb("modB", [P, KT])
        ss = sb("ss", [P, TT, 4])
        var = sb("var", [P, TT, 4])
        rs = sb("rs", [P, TT, 4])
        tn = sb("tn", [P, TT, 4])
        rstd = sb("rstd", [P, TT, 4])
        mx = sb("mx", [P, 2, GRP])
        sm = sb("sm", [P, 2, GRP])
        rsm = sb("rsm", [P, 2, GRP])
        eps = sb("eps", [P, 1])
        rows = vs[0:N_MOD + 4, :, :]
        sqr = vs[:, :, D - 2 * S:D - S]
        rqk = vs[:, :, D - S:D]
        ptf = pT[:, :, :, :].rearrange("p b h t -> p (b h t)")
        score = ptf[:, 0:S]
        selb = ptf[:, S:S + TT * S].rearrange("p (t s) -> p t s", t=TT)
        silu = eb[:, 0:2 * S]
        guf = eb[:, 2 * S:4 * S]
        zf = hTf[:, :, :].rearrange("p k s -> p (k s)")
        z0 = zf[:, 0:GRP * S].rearrange("p (h s) -> p h s", h=GRP)
        z1 = zf[:, GRP * S:GRP * (S + P)].rearrange("p (h s) -> p h s", h=GRP)
        e0 = eb[:, 0:GRP * S].rearrange("p (h s) -> p h s", h=GRP)
        e1 = eb[:, GRP * S:GRP * (S + P)].rearrange("p (h s) -> p h s", h=GRP)
        disti = hTf[:, 0, :].bitcast(I32)
        dm4 = hTf[:, 1, :].bitcast(I32)
        dm16 = hTf[:, 2, :].bitcast(I32)
        strict_i = hTf[:, 3, :].bitcast(I32)
        upper_i = hTf[:, 4, 0:P].bitcast(I32)
        ident_i = hTf[:, 5, 0:P].bitcast(I32)
        distf = xn[:, 0, 0:S]
        ge0 = xn[:, 0, S:2 * S]
        tmpf = xn[:, 0, 2 * S:3 * S]
        maskC = xn[:, 0, 3 * S:4 * S]

        PS = [ctx.enter_context(nc.psum_tensor(f"bank{i}", [P, HALF], F32)) for i in range(8)]
        DB = PS[0:4]
        GB, UB0, UB1, SB_ = PS[4], PS[5], PS[6], PS[7]
        PROJ = [PS[0], PS[1], PS[7]]
        EVEN, ODD, SSB, TRB, PVB = PS[3], PS[4], PS[2], PS[5], PS[6]

        raw_full = [sem(f"raw_full{k}") for k in range(NSLOT)]
        hi_full = [sem(f"hi_full{k}") for k in range(NSLOT)]
        split_done = [sem(f"split_done{k}") for k in range(NSLOT)]
        ada_full = [sem(f"ada_full{k}") for k in range(2)]
        ada_used = [sem(f"ada_used{k}") for k in range(2)]
        acc_ready = sem("acc_ready")
        modc_done = sem("modc_done")
        diag_ready = sem("diag_ready")
        gate_done = sem("gate_done")
        x_in = sem("x_in")
        rows_in = sem("rows_in")
        gains_in = sem("gains_in")
        c_in = sem("c_in")
        iotas = sem("iotas")
        tables = sem("tables")
        silu_c = sem("silu_c")
        cols_done = sem("cols_done")
        x_out = sem("x_out")
        sumsq = sem("sumsq")
        var_ready = sem("var_ready")
        rs_ready = sem("rs_ready")
        xn_ready = sem("xn_ready")
        tp_done = sem("tp_done")
        hTf_ready = sem("hTf_ready")
        hhi_ready = sem("hhi_ready")
        h_ready = sem("h_ready")
        out_done = sem("out_done")
        gate_ready = sem("gate_ready")
        g_done = sem("g_done")
        silu_ready = sem("silu_ready")
        u_done = sem("u_done")
        gu_ready = sem("gu_ready")
        guhi_ready = sem("guhi_ready")
        gulo_ready = sem("gulo_ready")
        d_done = sem("d_done")
        x_ready = sem("x_ready")
        proj_done = sem("proj_done")
        proj_act = sem("proj_act")
        proj_dve = sem("proj_dve")
        sq_ready = sem("sq_ready")
        ssq_done = sem("ssq_done")
        rqk_ready = sem("rqk_ready")
        pair_done = sem("pair_done")
        rel_read = sem("rel_read")
        rel_used = sem("rel_used")
        pair_read = sem("pair_read")
        logits_ready = sem("logits_ready")
        exps_ready = sem("exps_ready")
        probs_ready = sem("probs_ready")
        tr_done = sem("tr_done")
        pT_ready = sem("pT_ready")
        pv_done = sem("pv_done")
        o_read = sem("o_read")
        ln_ready = sem("ln_ready")
        log1m_ready = sem("log1m_ready")
        cum_done = sem("cum_done")
        zc_ready = sem("zc_ready")
        a_ready = sem("a_ready")

        block = ctx.enter_context(nc.Block())

        PAIRS = ["rel0", "rel1", "rel2", "A0", "A1", "Z0", "Z1", "C00", "C01", "C10", "C11"]
        SOFT = ["A0", "A1", "C00", "C01", "C10", "C11"]
        CJOBS = [s for s in SOFT if s[0] == "C"]
        TRS = [(s, b) for s in SOFT for b in range(int(s[-1]) + 1)]
        PVS = ["A0", "A1", "B0", "B1", "C00", "C01", "C10", "C11"]
        LATE = ("C01", "C11")

        PV_ORDER = ["A0", "A1", "B0", "B1", "C00", "C01", "C10", "C11"]
        PAIR_READS = PAIRS[3:]
        TPB = ((PS[4], PS[5]), (PS[6], PS[0]))
        GATES = ((PS[4], PS[5]), (PS[7], PS[2]), (PS[4], PS[5]))
        CUM = (PS[2], PS[5], PS[7])

        def in_pair(job):
            return (PS[0], PS[1]) if job in LATE else (EVEN, ODD)

        def width(job):
            return P * (int(job[-1]) + 1)

        def logits_of(job):
            return LG[SOFT.index(job) % 2][:, 0:GRP * width(job)].rearrange("p (h s) -> p h s", h=GRP)

        def chunk_cols(w, n=CW):
            return w[:, :].rearrange("p (k n) -> p k n", k=8)[:, :, 0:n]

        def at_cols(start, n):
            return slice(start, start + n) if isinstance(start, int) else bass.ds(start, n)

        def turn(l, n):
            return l * U_LAYER + n

        def nth(l, per_layer, n):
            return l * per_layer + n

        def ada_turn(l, slot, n):
            return ADA_PRE + l * ADA_TURNS[slot] + n

        MODC_PRE = AHEAD // 2
        MODC_L = NF + 1 + NF
        ACC_L = NF + MID + NF

        NB = 3
        NN = 4 * TT
        NORM_AT = {0: 0, 1: 1, 3: 2, 2: 3}

        @block.sync
        def _(sp):
            sp.dma_start(cT[:, :], c.rearrange("b (k p) -> p (b k)", p=P), allow_slow_non_contiguous=True).then_inc(c_in, 16)
            sp.dma_start(xs[:, :, :], x_v).then_inc(x_in, 16)
            sp.dma_start(rows[0:N_MOD, :, :], b_ada.rearrange("l (m d) -> m l d", d=D)).then_inc(rows_in, 16)
            for n, g in enumerate((norm_ffn1, norm_mix, norm_ffn2, g_out)):
                sp.dma_start(rows[N_MOD + n:N_MOD + n + 1, :, :], g.rearrange("(a l) d -> a l d", a=1)).then_inc(rows_in, 16)
            for n, g in enumerate((qn_a, kn_a, qn_c, kn_c)):
                for half in range(2):
                    sp.dma_start(qkg[half * HD:half * HD + HD, :, n], g.rearrange("l p -> p l"),
                                 allow_slow_non_contiguous=True).then_inc(gains_in, 16)

            def fill(slot, use, dst, src, waited=False):
                if not waited:
                    sp.wait_ge(split_done[slot], use + 1)
                sp.dma_start(dst, src).then_inc(raw_full[slot], 16)

            def ffn(l, base, wg, wu, wd):
                with sp.Fori(0, NF) as i:
                    use, k0, f0, r0 = (sp.snap(v) for v in (turn(l, base) + i, l * KT, i * CW, l * FT + i * 2))
                    fill(0, use, chunk_cols(raw[0]), wg[:, bass.ds(k0, KT), bass.ds(f0, CW)])
                    fill(1, use, chunk_cols(raw[1]), wu[:, bass.ds(k0, KT), bass.ds(f0, CW)])
                    fill(2, use, raw[2][:, :].rearrange("p (k n) -> p k n", k=2), wd[:, bass.ds(r0, 2), :])

            with sp.Fori(0, L) as l:
                ffn(l, U_FFN[0], v_gate, v_up, v_down)
                k_in = sp.snap(l * KT)
                for n, (kind, part) in enumerate(CHUNKS):
                    w = HD + H_I if kind == "ki" else CW
                    col = at[kind] + part * CW
                    if n == NSLOT:
                        for slot in range(2):
                            sp.wait_ge(split_done[slot], turn(l, U_IN + 1) + 1)
                    fill(n % NSLOT, turn(l, U_IN + n // NSLOT), chunk_cols(raw[n % NSLOT], w),
                         v_in[:, bass.ds(k_in, KT), col:col + w], waited=n in (NSLOT, NSLOT + 1))
                for n, (k0, nk) in enumerate(OUT_CHUNKS):
                    fill(n % NSLOT, turn(l, U_OUT + n // NSLOT),
                         raw[n % NSLOT][:, 0:nk * D].rearrange("p (k n) -> p k n", k=nk), v_out[:, bass.ds(l * KT + k0, nk), :])
                ffn(l, U_FFN[1], v_gate2, v_up2, v_down2)
            for t in range(TT):
                sp.wait_ge(x_ready, NB * TT * L + t + 1)
                sp.dma_start(out_v[:, t, :], xs[:, t, :]).then_inc(x_out, 16)
            sp.wait_ge(x_out, 16 * TT)

        @block.gpsimd
        def _(pool):
            pool.iota(disti, pattern=[[-1, S]], base=P, channel_multiplier=1).then_inc(iotas, 1)
            pool.iota(strict_i, pattern=[[1, S]], base=0, channel_multiplier=-1).then_inc(iotas, 1)
            pool.iota(upper_i, pattern=[[-1, P]], base=0, channel_multiplier=1).then_inc(iotas, 1)

            def fill(slot, turn_, row, col):
                pool.wait_ge(ada_used[slot], turn_)
                pool.dma_start(ada[:, slot, :, :], v_ada[:, row, col]).then_inc(ada_full[slot], 16)

            for m in range(AHEAD):
                fill(m % 2, m // 2 + 1, slice(0, KT), slice(m * CW, (m + 1) * CW))
            with pool.Fori(0, L) as l:
                rows_l = pool.snap(l * KT)
                with pool.Fori(0, NF) as i:
                    for k in range(2):
                        fill(k, ada_turn(l, k, i + 1), bass.ds(rows_l, KT), bass.ds(i * (2 * CW) + (AHEAD + k) * CW, CW))
                for n in range(MID):
                    m = AHEAD + 2 * NF + n
                    fill(n % 2, ada_turn(l, n % 2, NF + n // 2 + 1), bass.ds(rows_l, KT), slice(m * CW, (m + 1) * CW))
                with pool.Fori(0, NF - AHEAD) as i:
                    fill(0, ada_turn(l, 0, NF + 2 + i + 1), bass.ds(rows_l, KT), bass.ds(i * CW + (ADA_L - (NF - AHEAD)) * CW, CW))
                rows_n = pool.snap((l + 1) % L * KT)
                with pool.Fori(0, AHEAD) as i:
                    fill(0, ada_turn(l, 0, NF + 2 + NF - AHEAD + i + 1), bass.ds(rows_n, KT), bass.ds(i * CW, CW))

        @block.scalar
        def _(act):
            act.wait_ge(c_in, 16)
            act.activation(cT[:, :], cT[:, :], ACT.Silu).then_inc(silu_c, 1)

            def split_hi(slot, use, pieces=None):
                act.wait_ge(raw_full[slot], (use + 1) * 16)
                if pieces is None:
                    pieces = [(whi[slot][:, :], raw[slot][:, :])]
                for dst, src in pieces:
                    last = act.activation(dst, src, ACT.Copy)
                last.then_inc(hi_full[slot], 1)

            def root(l, n, t, groups):
                act.wait_ge(var_ready, nth(l, NN, NORM_AT[n] * TT + t + 1))
                act.activation(rs[:, t, 0:groups], var[:, t, 0:groups], ACT.Ln)
                act.drain()
                act.activation(rs[:, t, 0:groups], rs[:, t, 0:groups], ACT.Exp, scale=-0.5).then_inc(rs_ready, 1)

            def boundary(l, n, x_done):
                for t in range(TT):
                    act.wait_ge(x_ready, x_done + t + 1)
                    act.activation(xn[:, t, :], xs[:, t, :], ACT.Square, accum_out=ss[:, t, 0:1]).then_inc(sumsq, 1)
                    root(l, n, t, 1)
                high_of_h(l, n)

            def copy_gate(l, n):
                act.wait_ge(gate_done, nth(l, NB, n + 1))
                for half in range(2):
                    act.activation(gate[:, half * HALF:(half + 1) * HALF], GATES[n][half][:, :], ACT.Copy,
                                   scale=1.0 if n == 1 else 0.5).then_inc(gate_ready, 1)

            def high_of_h(l, n):
                for t in range(TT):
                    act.wait_ge(hTf_ready, nth(l, NN, NORM_AT[n] * TT + t + 1))
                    act.activation(hhi[:, :, t * P:(t + 1) * P], hTf[:, :, t * P:(t + 1) * P], ACT.Copy).then_inc(hhi_ready, 1)

            def ffn_step(l, which, i, ahead):
                base = turn(l, U_FFN[which])
                n = nth(l, 2 * NF, which * NF) + i
                act.wait_ge(g_done, n + 1)
                act.activation(silu, GB[:, :], ACT.Silu).then_inc(silu_ready, 1)
                split_hi(2, base + i)
                for ft in range(2):
                    act.wait_ge(gu_ready, n * 2 + ft + 1)
                    act.activation(guhi[:, ft * S:(ft + 1) * S], guf[:, ft * S:(ft + 1) * S], ACT.Copy).then_inc(guhi_ready, 1)
                    if ahead:
                        split_hi(ft, base + i + 1)

            def ffn(l, which):
                with act.Fori(0, NF - 1) as i:
                    ffn_step(l, which, i, True)
                ffn_step(l, which, NF - 1, False)

            def mix_split(l, n):
                slot = n % NSLOT
                pieces = None
                if CHUNKS[n][0] == "ki":
                    r = chunk_cols(raw[slot])
                    w = chunk_cols(whi[slot])
                    pieces = [(w[:, :, 0:HD], r[:, :, 0:HD]), (w[:, :, HD:2 * HD], r[:, :, 0:HD]),
                              (w[:, :, P:P + H_I], r[:, :, HD:HD + H_I])]
                split_hi(slot, turn(l, U_IN + n // NSLOT), pieces)

            def evacuate(l, n):
                kind, part = CHUNKS[n]
                bank = PROJ[n % 3]
                act.wait_ge(proj_done, nth(l, NC, n + 1))
                if n in NORMED:
                    act.activation(sqr, bank[:, :].rearrange("p (a s) -> p a s", a=2), ACT.Square).then_inc(sq_ready, 1)
                    return
                both = bank[:, :].rearrange("p (a s) -> p a s", a=2)
                if n == NC - 1:
                    act.wait_ge(proj_dve, nth(l, len(NORMED), len(NORMED)))
                if kind == "qi":
                    last = act.activation(qk1[:, 2 * part:2 * part + 2, :], both, ACT.Copy)
                elif kind == "ki":
                    act.activation(kiT[:, :], bank[:, 0:S], ACT.Copy)
                    last = act.activation(wi[:, :, :], bank[:, S:S + TT * H_I].rearrange("p (t h) -> p t h", t=TT), ACT.Copy)
                elif kind in ("qb", "kb"):
                    last = act.activation((qbT if kind == "qb" else kbT)[:, :, :], both, ACT.Copy)
                else:
                    off = {"va": 0, "vb": H_A * HD, "vc": (H_A + H_B) * HD}[kind] + part * CW
                    last = act.activation(vs[:, :, off:off + CW], both, ACT.Copy)
                last.then_inc(proj_act, 1)

            def inv_rms(l, n):
                j = NORMED.index(n)
                act.wait_ge(ssq_done, nth(l, len(NORMED), j + 1))
                if j >= 1:
                    act.wait_ge(proj_dve, nth(l, len(NORMED), j))
                act.activation(rqk, SSB[:, :].rearrange("p (a s) -> p a s", a=2), ACT.Ln, scale=1.0 / HD, bias=eps[:, :])
                act.drain()
                act.activation(rqk, rqk, ACT.Exp, scale=-0.5).then_inc(rqk_ready, 1)

            def rel_relu(l, j):
                act.wait_ge(pair_done, nth(l, len(PAIRS), j + 1))
                if j >= 2:
                    act.wait_ge(rel_used, nth(l, 3, j - 1))
                for odd in range(2):
                    last = act.activation(LG[j % 2][:, odd * HALF:(odd + 1) * HALF], (EVEN, ODD)[odd][:, :], ACT.Relu)
                last.then_inc(rel_read, 1)

            def exps(l, job):
                j = SOFT.index(job)
                act.wait_ge(logits_ready, nth(l, len(SOFT), j + 1))
                lg = logits_of(job)
                for h in range(GRP):
                    last = act.activation(lg[:, h, :], lg[:, h, :], ACT.Exp, bias=mx[:, j % 2, h:h + 1],
                                          **({"accum_out": sm[:, j % 2, h:h + 1]} if job[0] == "A" else {}))
                last.then_inc(exps_ready, 1)

            def copy_pT(l, job):
                for b in range(int(job[-1]) + 1):
                    n = TRS.index((job, b))
                    act.wait_ge(tr_done, nth(l, len(TRS), n + 1))
                    act.activation(pT[:, b, :, :], TRB[:, :].rearrange("p (h t) -> p h t", h=GRP), ACT.Copy).then_inc(pT_ready, 1)

            def softplus_log(l, st):
                z, e = ((z0, e0), (z1, e1))[st]
                act.wait_ge(pair_read, nth(l, 8, PAIR_READS.index(f"Z{st}") + 1))
                act.activation(e, z, ACT.Abs)
                act.drain()
                act.activation(e, e, ACT.Exp, scale=-1.0)
                act.drain()
                act.activation(e, e, ACT.Ln, bias=1.0).then_inc(ln_ready, 1)

            def stick_exps(l):
                for j in range(3):
                    act.wait_ge(zc_ready, nth(l, 3, j + 1))
                    part = z1 if j == 2 else z0[:, 2 * j:2 * j + 2, :]
                    act.activation(part, part, ACT.Exp).then_inc(a_ready, 1)

            act.wait_ge(tables, 2)
            act.wait_ge(x_in, 16)
            with act.Fori(0, L) as l:
                act.preload_act_table_set("natural_log_exp_and_others")
                boundary(l, 0, nth(l, NB * TT, 0))
                for k in range(2):
                    split_hi(k, turn(l, U_FFN[0]))
                ffn(l, 0)
                copy_gate(l, 0)
                act.preload_act_table_set("natural_log_exp_and_others")
                boundary(l, 1, nth(l, NB * TT, TT))
                mix_split(l, 0)
                mix_split(l, 1)
                for n in range(NC + 1):
                    if n >= 2 and n - 2 in NORMED:
                        inv_rms(l, n - 2)
                    if n >= 1:
                        evacuate(l, n - 1)
                    if n + 2 < NC:
                        mix_split(l, n + 2)
                    if n in (4, 5, 6):
                        rel_relu(l, n - 4)
                    if n == 9:
                        exps(l, "A0")
                    if n == 10:
                        exps(l, "A1")
                    if n in (11, 12):
                        softplus_log(l, n - 11)
                    if n == 12:
                        copy_pT(l, "A0")
                stick_exps(l)
                exps(l, "C00")
                copy_pT(l, "A1")
                exps(l, "C01")
                copy_pT(l, "C00")
                exps(l, "C10")
                copy_pT(l, "C01")
                exps(l, "C11")
                for k in range(NSLOT):
                    split_hi(k, turn(l, U_OUT), [(whi[k][:, 0:D], raw[k][:, 0:D])])
                copy_pT(l, "C10")
                copy_pT(l, "C11")
                copy_gate(l, 1)
                for t in range(TT):
                    act.wait_ge(o_read, nth(l, len(PVS), len(PVS) - 1 + t))
                    for g, (a, b) in enumerate(((0, 256), (256, 512), (512, 1024))):
                        last = act.activation(eb[:, a:b], xn[:, t, a:b], ACT.Square, accum_out=ss[:, t, g:g + 1])
                    last.then_inc(sumsq, 1)
                    root(l, 3, t, 3)
                high_of_h(l, 3)
                for n in range(NSLOT, len(OUT_CHUNKS)):
                    k = n % NSLOT
                    nk = OUT_CHUNKS[n][1]
                    act.wait_ge(out_done, nth(l, len(OUT_CHUNKS), n - NSLOT + 1))
                    split_hi(k, turn(l, U_OUT + 1), [(whi[k][:, 0:nk * D], raw[k][:, 0:nk * D])])
                boundary(l, 2, nth(l, NB * TT, 2 * TT))
                for k in range(2):
                    split_hi(k, turn(l, U_FFN[1]))
                ffn(l, 1)
                copy_gate(l, 2)

        @block.vector
        def _(dve):
            for k in range(NSLOT):
                dve.sem_inc(split_done[k], 1)
            for k in range(2):
                dve.sem_inc(ada_used[k], 1)
            dve.memset(zero16[:, :], 0.0)
            dve.memset(ones[:, :], 1.0)
            dve.memset(heads1[:, :], 0.0)
            dve.memset(eps[:, :], EPS)
            dve.drain()
            for k in range(2):
                dve.memset(heads1[k * HD:(k + 1) * HD, k * HD:(k + 1) * HD], 1.0)
            dve.wait_ge(iotas, 3)
            dve.tensor_scalar(ident[:, :], upper_i, 0.0, None, ALU.is_equal)
            dve.tensor_scalar(upper[:, :], upper_i, 0.0, None, ALU.is_ge).then_inc(tables, 1)
            dve.tensor_scalar(strictT[:, :], strict_i, 0.0, NEG, ALU.is_le, ALU.mult)
            dve.tensor_scalar(dm4, disti, DILATIONS[1][1] - 1, None, ALU.bitwise_and)
            dve.tensor_scalar(dm16, disti, DILATIONS[2][1] - 1, None, ALU.bitwise_and)
            dve.tensor_copy(distf, disti)
            dve.drain()
            dve.tensor_scalar(ge0, distf, 0.0, None, ALU.is_ge)
            dve.tensor_scalar(causal[:, :], distf, 0.0, NEG, ALU.is_lt, ALU.mult)
            dve.tensor_scalar(tmpf, dm4, 0.0, None, ALU.is_equal)
            dve.tensor_scalar(maskC, dm16, 0.0, None, ALU.is_equal)
            dve.drain()
            dve.tensor_tensor(tmpf, tmpf, maskC, ALU.add)
            dve.drain()
            dve.scalar_tensor_tensor(mult[:, :], distf, float(DILATIONS[0][0]), tmpf, ALU.is_le, ALU.add)
            dve.drain()
            dve.tensor_tensor(mult[:, :], mult[:, :], ge0, ALU.mult)
            dve.drain()
            dve.tensor_scalar(maskC, mult[:, :], 0.0, NEG, ALU.is_equal, ALU.mult)
            dve.drain()
            s_a, s_c = slopes()
            for h in range(H_A):
                dve.scalar_tensor_tensor(aliA[:, h, :], distf, -s_a[h], causal[:, :], ALU.mult, ALU.add)
            for h in range(H_C):
                dve.scalar_tensor_tensor(aliC[:, h, :], distf, -s_c[h], maskC, ALU.mult, ALU.add)
            dve.wait_ge(cols_done, 1)
            dve.tensor_copy(cols[:, :, :, :], PS[0][:, 0:L * KT * 13].rearrange("p (l k m) -> p l k m", l=L, k=KT))
            dve.wait_ge(x_in, 16)
            dve.sem_inc(x_ready, TT)
            dve.wait_ge(gains_in, 8 * 16)
            dve.drain().then_inc(tables, 1)

            def weigh_ada(turns, slots):
                for slot, n in zip(slots, turns):
                    dve.wait_ge(ada_full[slot], n * 16)
                a, b = slots[0], slots[-1] + 1
                for k in range(KT):
                    if k == 0:
                        dve.tensor_scalar(acc[:, a:b, :], ada[:, a:b, k, :], cT[:, 0:1], None, ALU.mult)
                    else:
                        last = dve.scalar_tensor_tensor(acc[:, a:b, :], ada[:, a:b, k, :], cT[:, k:k + 1], acc[:, a:b, :], ALU.mult, ALU.add)
                    if k < KT - 1:
                        dve.drain()
                last.then_inc(acc_ready, 1)
                for slot in slots:
                    dve.drain().then_inc(ada_used[slot], 1)

            def read_modc(done, dst, bank):
                dve.wait_ge(modc_done, done)
                dve.tensor_copy(dst, bank)

            def diagonal(n):
                off = (3 * n + 2) * KT
                dve.drain()
                dve.tensor_tensor(modc[:, off:off + KT], modc[:, off:off + KT], biasL[:, 3 * n + 2, :], ALU.add)
                dve.drain()
                for k in range(KT):
                    last = dve.tensor_scalar(gate[:, k * P:(k + 1) * P], ident[:, :], modc[:, off + k:off + k + 1], None, ALU.mult)
                last.then_inc(diag_ready, 1)

            def split_lo(slot, use, pieces=None):
                dve.wait_ge(hi_full[slot], use + 1)
                if pieces is None:
                    pieces = [(wlo[slot][:, :], raw[slot][:, :], whi[slot][:, :])]
                for dst, src, hi in pieces:
                    last = dve.tensor_tensor(dst, src, hi.bitcast(F32), ALU.subtract)
                last.then_inc(split_done[slot], 1)

            def refine(l, n, t, groups, counts):
                dve.wait_ge(sumsq, nth(l, NN, NORM_AT[n] * TT + t + 1))
                if len(set(counts)) == 1:
                    dve.tensor_scalar(var[:, t, 0:groups], ss[:, t, 0:groups], 1.0 / counts[0], EPS, ALU.mult, ALU.add).then_inc(var_ready, 1)
                else:
                    for g, m in enumerate(counts):
                        last = dve.tensor_scalar(var[:, t, g:g + 1], ss[:, t, g:g + 1], 1.0 / m, EPS, ALU.mult, ALU.add)
                    last.then_inc(var_ready, 1)
                dve.wait_ge(rs_ready, nth(l, NN, NORM_AT[n] * TT + t + 1))
                dve.tensor_tensor(tn[:, t, 0:groups], rs[:, t, 0:groups], rs[:, t, 0:groups], ALU.mult)
                dve.drain()
                dve.tensor_tensor(tn[:, t, 0:groups], tn[:, t, 0:groups], var[:, t, 0:groups], ALU.mult)
                dve.drain()
                dve.tensor_scalar(tn[:, t, 0:groups], tn[:, t, 0:groups], -0.5, 1.5, ALU.mult, ALU.add)
                dve.drain()
                dve.tensor_tensor(rstd[:, t, 0:groups], tn[:, t, 0:groups], rs[:, t, 0:groups], ALU.mult)
                dve.drain()

            def transposed(l, n, gain, shift):
                for t in range(TT):
                    for half in range(2):
                        dve.wait_ge(tp_done, nth(l, 4 * 2 * TT, (NORM_AT[n] * TT + t) * 2 + half + 1))
                        bank = TPB[t][half]
                        for k in range(4):
                            kk = half * 4 + k
                            last = dve.tensor_scalar(hTf[:, kk, t * P:(t + 1) * P], bank[:, k * P:(k + 1) * P], gain[:, kk:kk + 1],
                                                     None if shift is None else shift[:, kk:kk + 1], ALU.mult,
                                                     **({} if shift is None else {"op1": ALU.add}))
                    last.then_inc(hTf_ready, 1)
                for t in range(TT):
                    dve.wait_ge(hhi_ready, nth(l, NN, NORM_AT[n] * TT + t + 1))
                    tok = slice(t * P, (t + 1) * P)
                    dve.tensor_tensor(hlo[:, :, tok], hTf[:, :, tok], hhi[:, :, tok].bitcast(F32), ALU.subtract).then_inc(h_ready, 1)

            def boundary(l, n):
                for t in range(TT):
                    refine(l, n, t, 1, [D])
                    dve.tensor_scalar(xn[:, t, :], xs[:, t, :], rstd[:, t, 0:1], None, ALU.mult).then_inc(xn_ready, 1)
                off = 3 * n * KT
                dve.tensor_tensor(modB[:, :], modc[:, off:off + KT], biasL[:, 3 * n, :], ALU.add)
                dve.tensor_tensor(modA[:, :], modc[:, off + KT:off + 2 * KT], biasL[:, 3 * n + 1, :], ALU.add)
                dve.drain()
                dve.scalar_tensor_tensor(modA[:, :], modA[:, :], 1.0, colL[:, :, N_MOD + n], ALU.add, ALU.mult)
                dve.drain()
                transposed(l, n, modA, modB)

            def residual(l, n):
                for t in range(TT):
                    if t == 0:
                        dve.wait_ge(gate_ready, nth(l, 2 * NB, 2 * n + 2))
                        if n == 1:
                            dve.wait_ge(out_done, nth(l, len(OUT_CHUNKS), len(OUT_CHUNKS)))
                        else:
                            dve.wait_ge(d_done, nth(l, 2, n // 2 + 1))
                    for half in range(2):
                        cut = slice(half * HALF, (half + 1) * HALF)
                        dve.tensor_tensor(xn[:, t, cut], DB[2 * t + half][:, :], gate[:, cut], ALU.mult)
                    dve.drain()
                    dve.tensor_tensor(xs[:, t, :], xs[:, t, :], xn[:, t, :], ALU.add).then_inc(x_ready, 1)

            def ffn_step(l, which, i, ahead):
                base = turn(l, U_FFN[which])
                n = nth(l, 2 * NF, which * NF) + i
                if which == 0:
                    weigh_ada([ada_turn(l, k, i + 1) for k in range(2)], [0, 1])
                else:
                    weigh_ada([ada_turn(l, 0, NF + 2 + i + 1)], [0])
                split_lo(2, base + i)
                dve.wait_ge(silu_ready, n + 1)
                for ft in range(2):
                    cut = slice(ft * S, (ft + 1) * S)
                    dve.wait_ge(u_done, n * 2 + ft + 1)
                    dve.tensor_tensor(guf[:, cut], silu[:, cut], (UB0, UB1)[ft][:, 0:S], ALU.mult).then_inc(gu_ready, 1)
                    dve.wait_ge(guhi_ready, n * 2 + ft + 1)
                    dve.tensor_tensor(gulo[:, cut], guf[:, cut], guhi[:, cut].bitcast(F32), ALU.subtract).then_inc(gulo_ready, 1)
                if which == 0:
                    read_modc(MODC_PRE + nth(l, MODC_L, 1) + i, modc[:, at_cols(AHEAD * CT + i * (2 * CT), 2 * CT)], SB_[:, 0:2 * CT])
                else:
                    read_modc(MODC_PRE + nth(l, MODC_L, NF + 2) + i, modc[:, at_cols((AHEAD + 2 * NF + MID) * CT + i * CT, CT)], SB_[:, 0:CT])
                if ahead:
                    for k in range(2):
                        split_lo(k, base + i + 1)

            def ffn(l, which):
                with dve.Fori(0, NF - 1) as i:
                    ffn_step(l, which, i, True)
                ffn_step(l, which, NF - 1, False)
                diagonal(2 * which)

            def mix_split(l, n):
                slot = n % NSLOT
                pieces = None
                if CHUNKS[n][0] == "ki":
                    r, w, v = chunk_cols(raw[slot]), chunk_cols(whi[slot]), chunk_cols(wlo[slot])
                    pieces = [(v[:, :, 0:HD], r[:, :, 0:HD], w[:, :, 0:HD]), (v[:, :, HD:2 * HD], r[:, :, 0:HD], w[:, :, HD:2 * HD]),
                              (v[:, :, P:P + H_I], r[:, :, HD:HD + H_I], w[:, :, P:P + H_I])]
                split_lo(slot, turn(l, U_IN + n // NSLOT), pieces)

            def head_norm(l, n):
                kind, part = CHUNKS[n]
                j = NORMED.index(n)
                dve.wait_ge(rqk_ready, nth(l, len(NORMED), j + 1))
                dst = {"qa": qk2[:, 0:2, :], "ka": qk2[:, 2:4, :], "qc": qk2[:, 2 * part:2 * part + 2, :],
                       "kc": qk1[:, 2 * part:2 * part + 2, :]}[kind]
                both = lambda a: a.rearrange("p (a s) -> p a s", a=2)
                dve.scalar_tensor_tensor(dst, both(PROJ[n % 3][:, :]), qkgL[:, GAIN[kind]:GAIN[kind] + 1], rqk,
                                         ALU.mult, ALU.mult).then_inc(proj_dve, 1)

            def weigh(l, j):
                dve.wait_ge(rel_read, nth(l, 3, j + 1))
                t = 0 if j == 0 else 1
                w = P * (t + 1)
                n_heads = 8 if j == 0 else 4
                for h in range(n_heads):
                    head = h + (4 if j == 2 else 0)
                    src = LG[j % 2][:, (h % 2) * HALF + (h // 2) * w:(h % 2) * HALF + (h // 2 + 1) * w]
                    if head == 0:
                        last = dve.tensor_scalar(score[:, 0:w], src, wi[:, t, 0:1], None, ALU.mult)
                    else:
                        last = dve.scalar_tensor_tensor(score[:, 0:w], src, wi[:, t, head:head + 1], score[:, 0:w], ALU.mult, ALU.add)
                    if h == n_heads - 1:
                        last.then_inc(rel_used, 1)
                    dve.drain()
                if j != 1:
                    dve.scalar_tensor_tensor(score[:, 0:w], score[:, 0:w], HD ** -0.5 * H_I ** -0.5, causal[:, S - w:S], ALU.mult, ALU.add)
                    dve.drain()

            def take_top(t, rounds):
                w = P * (t + 1)
                for _ in range(rounds):
                    dve.max(top8[:, :], score[:, 0:w])
                    dve.drain()
                    dve.match_replace(score[:, 0:w], top8[:, :], score[:, 0:w], TAKEN)
                    dve.drain()

            def select(t):
                w = P * (t + 1)
                dve.tensor_scalar(selb[:, t, 0:w], score[:, 0:w], TAKEN, NEG, ALU.not_equal, ALU.mult)
                dve.drain()

            def logits(l, job):
                j = SOFT.index(job)
                w = width(job)
                lg = logits_of(job)
                even, odd = in_pair(job)
                bias = aliA if job[0] == "A" else aliC[:, GRP * int(job[1]):GRP * (int(job[1]) + 1), :]
                dve.wait_ge(pair_done, nth(l, len(PAIRS), PAIRS.index(job) + 1))
                if j >= 2:
                    dve.wait_ge(tr_done, nth(l, len(TRS), TRS.index((SOFT[j - 2], int(SOFT[j - 2][-1]))) + 1))
                for odd_, bank in enumerate((even, odd)):
                    last = dve.scalar_tensor_tensor(lg[:, odd_::2, :], bank[:, 0:2 * w].rearrange("p (h s) -> p h s", h=2), HD ** -0.5,
                                                    bias[:, odd_::2, S - w:S], ALU.mult, ALU.add)
                last.then_inc(pair_read, 1)
                dve.drain()
                if job[0] == "A":
                    t = int(job[-1])
                    dve.tensor_tensor(lg, lg, selb[:, t:t + 1, 0:w].to_broadcast([P, GRP, w]), ALU.add)
                    dve.drain()
                dve.tensor_reduce(mx[:, j % 2, :], lg, AX_X, ALU.max)
                dve.drain()
                dve.tensor_scalar(mx[:, j % 2, :], mx[:, j % 2, :], -1.0, None, ALU.mult).then_inc(logits_ready, 1)

            def weigh_probs(l, job):
                j = SOFT.index(job)
                w = width(job)
                lg = logits_of(job)
                dve.wait_ge(exps_ready, nth(l, len(SOFT), j + 1))
                for h in range(GRP):
                    last = dve.scalar_tensor_tensor(lg[:, h, :], lg[:, h, :], 1.0, mult[:, S - w:S], ALU.mult, ALU.mult,
                                                    accum_out=sm[:, j % 2, h:h + 1])
                last.then_inc(probs_ready, 1)
                dve.drain()

            def read_out(l, job):
                t = int(job[-1])
                off = {"A": 0, "B": H_A * HD}.get(job[0], (H_A + H_B) * HD + (int(job[1]) * GRP * HD if job[0] == "C" else 0))
                if job[0] != "B":
                    j = SOFT.index(job)
                    if job[0] == "A":
                        dve.wait_ge(exps_ready, nth(l, len(SOFT), j + 1))
                    dve.reciprocal(rsm[:, j % 2, :], sm[:, j % 2, :])
                    dve.drain()
                dve.wait_ge(pv_done, nth(l, len(PVS), PV_ORDER.index(job) + 1))
                dst = xn[:, t, off:off + GRP * HD]
                src = PVB[:, 0:GRP * HD]
                if job[0] == "B":
                    dve.tensor_copy(dst, src).then_inc(o_read, 1)
                else:
                    dve.tensor_tensor(dst.rearrange("p (h d) -> p h d", h=GRP), src.rearrange("p (h d) -> p h d", h=GRP),
                                      rsm[:, j % 2, :].unsqueeze(2).to_broadcast([P, GRP, HD]), ALU.mult).then_inc(o_read, 1)

            def stick_logits(l, st):
                z = (z0, z1)[st]
                w = S - st * P
                dve.wait_ge(pair_done, nth(l, len(PAIRS), PAIRS.index(f"Z{st}") + 1))
                for odd_, bank in enumerate((EVEN, ODD)):
                    last = dve.scalar_tensor_tensor(z[:, odd_::2, :], bank[:, 0:2 * w].rearrange("p (h s) -> p h s", h=2), HD ** -0.5,
                                                    strictT[:, 0:w].unsqueeze(1).to_broadcast([P, 2, w]), ALU.mult, ALU.add)
                last.then_inc(pair_read, 1)

            def softplus(l, st):
                z, e = ((z0, e0), (z1, e1))[st]
                dve.wait_ge(ln_ready, nth(l, 2, st + 1))
                dve.scalar_tensor_tensor(e, z, 0.0, e, ALU.max, ALU.add).then_inc(log1m_ready, 1)

            def minus_cum(l):
                for j in range(3):
                    part = z1 if j == 2 else z0[:, 2 * j:2 * j + 2, :]
                    dve.wait_ge(cum_done, nth(l, 3, j + 1))
                    dve.tensor_tensor(part, part, CUM[j][:, :].rearrange("p (h s) -> p h s", h=4 if j == 2 else 2), ALU.subtract).then_inc(zc_ready, 1)

            dve.wait_ge(silu_c, 1)
            for n in range(AHEAD // 2):
                weigh_ada([n + 1, n + 1], [0, 1])
                read_modc(n + 1, modc[:, N_MOD * KT + 2 * CT * n:N_MOD * KT + 2 * CT * (n + 1)], SB_[:, 0:2 * CT])
                dve.drain()
            with dve.Fori(0, L) as l:
                dve.tensor_copy(colL[:, :, :], cols[:, bass.ds(l, 1), :, :].rearrange("p a k m -> p (a k) m"))
                dve.tensor_copy(modc[:, 0:2 * KT], modc[:, N_MOD * KT:(N_MOD + 2) * KT])
                dve.tensor_copy(biasL[:, :, :], cols[:, bass.ds(l, 1), :, 0:N_MOD].rearrange("p a k m -> p m (a k)"))
                dve.tensor_copy(qkgL[:, :], qkg[:, bass.ds(l, 1), :].rearrange("p a k -> p (a k)"))
                dve.drain()
                boundary(l, 0)
                for k in range(2):
                    split_lo(k, turn(l, U_FFN[0]))
                ffn(l, 0)
                residual(l, 0)
                boundary(l, 1)
                mix_split(l, 0)
                mix_split(l, 1)
                for n in range(NC + 1):
                    if n >= 2 and n - 2 in NORMED:
                        head_norm(l, n - 2)
                    if n + 2 < NC:
                        mix_split(l, n + 2)
                    if n < MID:
                        slot = n % 2
                        weigh_ada([ada_turn(l, slot, NF + n // 2 + 1)], [slot])
                        if n == MID - 1:
                            off = (AHEAD + 2 * NF) * CT
                            read_modc(MODC_PRE + nth(l, MODC_L, NF + 1), modc[:, off:off + MID * CT], PVB[:, 0:MID * CT])
                            diagonal(1)
                    if n == 4:
                        weigh(l, 0)
                        take_top(0, TOPK // 8)
                        select(0)
                    if n == 5:
                        weigh(l, 1)
                    if n == 6:
                        weigh(l, 2)
                        take_top(1, TOPK // 16)
                    if n == 7:
                        take_top(1, TOPK // 16)
                        select(1)
                    if n in (8, 9):
                        logits(l, f"A{n - 8}")
                    if n in (10, 11):
                        stick_logits(l, n - 10)
                    if n in (12, 13):
                        softplus(l, n - 12)
                    if n == 13:
                        read_out(l, "A0")
                minus_cum(l)
                logits(l, "C00")
                read_out(l, "A1")
                logits(l, "C01")
                weigh_probs(l, "C00")
                read_out(l, "B0")
                read_out(l, "B1")
                read_out(l, "C00")
                logits(l, "C10")
                weigh_probs(l, "C01")
                read_out(l, "C01")
                logits(l, "C11")
                weigh_probs(l, "C10")
                read_out(l, "C10")
                weigh_probs(l, "C11")
                read_out(l, "C11")
                for k in range(NSLOT):
                    split_lo(k, turn(l, U_OUT), [(wlo[k][:, 0:D], raw[k][:, 0:D], whi[k][:, 0:D])])
                for t in range(TT):
                    refine(l, 3, t, 3, [H_A * HD, H_B * HD, H_C * HD])
                    for g, (a, b) in enumerate(((0, 256), (256, 512), (512, 1024))):
                        last = dve.tensor_scalar(xn[:, t, a:b], xn[:, t, a:b], rstd[:, t, g:g + 1], None, ALU.mult)
                    last.then_inc(xn_ready, 1)
                transposed(l, 3, colL[:, :, 12], None)
                for n in range(NSLOT, len(OUT_CHUNKS)):
                    k = n % NSLOT
                    nk = OUT_CHUNKS[n][1]
                    split_lo(k, turn(l, U_OUT + 1), [(wlo[k][:, 0:nk * D], raw[k][:, 0:nk * D], whi[k][:, 0:nk * D])])
                residual(l, 1)
                boundary(l, 2)
                for k in range(2):
                    split_lo(k, turn(l, U_FFN[1]))
                ffn(l, 1)
                residual(l, 2)

        @block.tensor
        def _(pe):
            pe.wait_ge(tables, 1)
            pe.wait_ge(rows_in, 5 * 16)
            for l in range(L):
                for k in range(KT):
                    o = (l * KT + k) * 13
                    last = pe.transpose(PS[0][:, o:o + 13], rows[:, l, k * P:(k + 1) * P], ident[0:13, 0:13])
            last.then_inc(cols_done, 1)

            def three(ps, l_hi, l_lo, r_hi, r_lo, first, last):
                pe.matmul(ps, l_hi, r_hi, start=first, stop=False)
                pe.matmul(ps, l_hi, r_lo, start=False, stop=False)
                return pe.matmul(ps, l_lo, r_hi, start=False, stop=last)

            def sum_ada(ready, slots, bank, at_=0):
                pe.wait_ge(acc_ready, ready)
                for slot in slots:
                    for j in range(CT):
                        last = pe.matmul(bank[:, at_:at_ + 1], acc[:, slot, j * P:(j + 1) * P], ones[:, 0:1], start=True, stop=True)
                        at_ += 1
                return last

            def spread_gate(l, n):
                pe.wait_ge(diag_ready, nth(l, NB, n + 1))
                for half in range(2):
                    last = pe.matmul(GATES[n][half][:, :], ones[:, :], gate[:, half * HALF:(half + 1) * HALF], start=True, stop=True)
                last.then_inc(gate_done, 1)

            def turn_h(l, n):
                for t in range(TT):
                    pe.wait_ge(xn_ready, nth(l, NN, NORM_AT[n] * TT + t + 1))
                    for half in range(2):
                        for k in range(4):
                            kk = half * 4 + k
                            last = pe.transpose(TPB[t][half][:, k * P:(k + 1) * P], xn[:, t, kk * P:(kk + 1) * P], ident[:, :])
                        last.then_inc(tp_done, 1)

            def wait_h(l, n):
                pe.wait_ge(h_ready, nth(l, NN, (NORM_AT[n] + 1) * TT))

            def ffn(l, which):
                wait_h(l, 2 * which)
                for b in range(4):
                    pe.matmul(DB[b][:, :], zero16[:, 0:P], zero16[:, :], start=True, stop=False)
                with pe.Fori(0, NF) as i:
                    use = turn(l, U_FFN[which]) + i
                    n = nth(l, 2 * NF, which * NF) + i
                    pe.wait_ge(split_done[0], use + 2)
                    wh, wl = chunk_cols(whi[0]), chunk_cols(wlo[0])
                    for ft in range(2):
                        for k in range(KT):
                            last = three(GB[:, ft * S:(ft + 1) * S], wh[:, k, ft * P:(ft + 1) * P], wl[:, k, ft * P:(ft + 1) * P],
                                         hhi[:, k, :], hlo[:, k, :], k == 0, k == KT - 1)
                    last.then_inc(g_done, 1)
                    pe.wait_ge(split_done[1], use + 2)
                    wh, wl = chunk_cols(whi[1]), chunk_cols(wlo[1])
                    for ft in range(2):
                        for k in range(KT):
                            last = three((UB0, UB1)[ft][:, 0:S], wh[:, k, ft * P:(ft + 1) * P], wl[:, k, ft * P:(ft + 1) * P],
                                         hhi[:, k, :], hlo[:, k, :], k == 0, k == KT - 1)
                        last.then_inc(u_done, 1)
                    if which == 0:
                        sum_ada(nth(l, ACC_L, AHEAD // 2 + 1) + i, [0, 1], SB_).then_inc(modc_done, 1)
                    else:
                        sum_ada(nth(l, ACC_L, AHEAD // 2 + NF + MID + 1) + i, [0], SB_).then_inc(modc_done, 1)
                    pe.wait_ge(split_done[2], use + 2)
                    for ft in range(2):
                        pe.wait_ge(gulo_ready, n * 2 + ft + 1)
                        for t in range(TT):
                            tok = slice(ft * S + t * P, ft * S + (t + 1) * P)
                            for half in range(2):
                                w = slice(ft * D + half * HALF, ft * D + (half + 1) * HALF)
                                last = three(DB[2 * t + half][:, :], guhi[:, tok], gulo[:, tok], whi[2][:, w], wlo[2][:, w], False, False)
                for b in range(4):
                    last = pe.matmul(DB[b][:, :], zero16[:, 0:P], zero16[:, :], start=False, stop=True)
                last.then_inc(d_done, 1)
                spread_gate(l, 2 * which)

            def project(l, n):
                kind, part = CHUNKS[n]
                slot = n % NSLOT
                bank = PROJ[n % 3]
                pe.wait_ge(split_done[slot], turn(l, U_IN + n // NSLOT) + 2)
                if n >= 3:
                    if n - 3 in NORMED:
                        pe.wait_ge(proj_dve, nth(l, len(NORMED), NORMED.index(n - 3) + 1))
                    else:
                        pe.wait_ge(proj_act, nth(l, NC - len(NORMED), n - 3 - sum(m < n - 3 for m in NORMED) + 1))
                wh, wl = chunk_cols(whi[slot]), chunk_cols(wlo[slot])
                if kind[0] == "v":
                    for t in range(TT):
                        tok = slice(t * P, (t + 1) * P)
                        for k in range(KT):
                            last = three(bank[:, t * CW:(t + 1) * CW], hhi[:, k, tok], hlo[:, k, tok], wh[:, k, :], wl[:, k, :], k == 0, k == KT - 1)
                else:
                    for ct in range(1 if kind == "ki" else 2):
                        for k in range(KT):
                            cut = slice(ct * P, (ct + 1) * P)
                            last = three(bank[:, ct * S:(ct + 1) * S], wh[:, k, cut], wl[:, k, cut], hhi[:, k, :], hlo[:, k, :], k == 0, k == KT - 1)
                    if kind == "ki":
                        for t in range(TT):
                            tok = slice(t * P, (t + 1) * P)
                            for k in range(KT):
                                last = three(bank[:, S + t * H_I:S + (t + 1) * H_I], hhi[:, k, tok], hlo[:, k, tok],
                                             wh[:, k, P:P + H_I], wl[:, k, P:P + H_I], k == 0, k == KT - 1)
                last.then_inc(proj_done, 1)

            def sum_squares(l, n):
                j = NORMED.index(n)
                pe.wait_ge(sq_ready, nth(l, len(NORMED), j + 1))
                if j >= 1:
                    pe.wait_ge(rqk_ready, nth(l, len(NORMED), j))
                pe.matmul(SSB[:, :].rearrange("p (a s) -> p a s", a=2), heads1[:, :], sqr, start=True, stop=True).then_inc(ssq_done, 1)

            def pair(l, job, products):
                j = PAIRS.index(job)
                if job in LATE:
                    if job == "C01":
                        pe.wait_ge(proj_dve, nth(l, len(NORMED), len(NORMED)))
                        pe.wait_ge(proj_act, nth(l, NC - len(NORMED), NC - len(NORMED) - 1))
                    else:
                        pe.wait_ge(pair_read, nth(l, 8, PAIR_READS.index("C01") + 1))
                elif j >= 1:
                    before = PAIRS[j - 2] if job == "C10" else PAIRS[j - 1]
                    if before[:3] == "rel":
                        pe.wait_ge(rel_read, nth(l, 3, PAIRS.index(before) + 1))
                    else:
                        pe.wait_ge(pair_read, nth(l, 8, PAIR_READS.index(before) + 1))
                w = products[0][3]
                for n, (head, lhsT, rhs, w) in enumerate(products):
                    bank = in_pair(job)[head % 2]
                    last = pe.matmul(bank[:, (n // 2) * w:(n // 2 + 1) * w], lhsT, rhs, start=True, stop=True)
                last.then_inc(pair_done, 1)

            def head_rows(h):
                return slice((h % 2) * HD, (h % 2 + 1) * HD)

            def relevance(l, j):
                if j == 0:
                    pe.wait_ge(proj_act, nth(l, NC - len(NORMED), 3))
                t = 0 if j == 0 else 1
                tok = slice(t * P, (t + 1) * P)
                heads = {0: range(8), 1: range(4), 2: range(4, 8)}[j]
                w = P * (t + 1)
                pair(l, f"rel{j}", [(h, qk1[head_rows(h), h // 2, tok], kiT[head_rows(h), 0:w], w) for h in heads])

            def attend(l, job):
                t = int(job[-1])
                tok = slice(t * P, (t + 1) * P)
                w = width(job)
                if job == "A0":
                    pe.wait_ge(proj_dve, nth(l, len(NORMED), 2))
                if job == "C00":
                    pe.wait_ge(proj_dve, nth(l, len(NORMED), len(NORMED)))
                if job[0] == "A":
                    q, k = qk2[:, 0:2, :], qk2[:, 2:4, :]
                else:
                    g = int(job[1])
                    q, k = qk2[:, 2 * g:2 * g + 2, :], qk1[:, 2 * g:2 * g + 2, :]
                pair(l, job, [(h, q[head_rows(h), h // 2, tok], k[head_rows(h), h // 2, 0:w], w) for h in range(GRP)])

            def stick(l, st):
                if st == 0:
                    pe.wait_ge(proj_act, nth(l, NC - len(NORMED), 6))
                pair(l, f"Z{st}", [(h, kbT[head_rows(h), h // 2, st * P:(st + 1) * P], qbT[head_rows(h), h // 2, st * P:S], S - st * P)
                                   for h in range(GRP)])

            def cumulate(l):
                pe.wait_ge(log1m_ready, nth(l, 2, 2))
                pe.wait_ge(rqk_ready, nth(l, len(NORMED), len(NORMED)))
                pe.wait_ge(pT_ready, nth(l, len(TRS), 1))
                pe.wait_ge(proj_act, nth(l, NC - len(NORMED), NC - len(NORMED)))
                for j in range(2):
                    hs = slice(2 * j, 2 * j + 2)
                    both = CUM[j][:, :].rearrange("p (h s) -> p h s", h=2)
                    pe.matmul(both, upper[:, :], e0[:, hs, :], start=True, stop=False)
                    pe.matmul(both[:, :, P:S], ones[:, :], e1[:, hs, :], start=False, stop=True).then_inc(cum_done, 1)
                pe.matmul(CUM[2][:, :].rearrange("p (h s) -> p h s", h=4), upper[:, :], e1, start=True, stop=True).then_inc(cum_done, 1)

            def turn_probs(l, job):
                j = SOFT.index(job)
                lg = logits_of(job)
                if job[0] == "A":
                    pe.wait_ge(exps_ready, nth(l, len(SOFT), j + 1))
                else:
                    pe.wait_ge(probs_ready, nth(l, len(CJOBS), CJOBS.index(job) + 1))
                if job == "A1":
                    pe.wait_ge(zc_ready, nth(l, 3, 2))
                for b in range(int(job[-1]) + 1):
                    n = TRS.index((job, b))
                    if n >= 1:
                        pe.wait_ge(pT_ready, nth(l, len(TRS), n))
                    for h in range(GRP):
                        last = pe.transpose(TRB[:, h * P:(h + 1) * P], lg[:, h, b * P:(b + 1) * P], ident[:, :])
                    last.then_inc(tr_done, 1)

            def values(l, job):
                t = int(job[-1])
                n = PV_ORDER.index(job)
                if job[0] == "B":
                    pe.wait_ge(a_ready, nth(l, 3, 3))
                    off = H_A * HD
                    probs = lambda b, h: z1[:, h, :] if b == 1 else z0[:, h, t * P:(t + 1) * P]
                else:
                    pe.wait_ge(pT_ready, nth(l, len(TRS), TRS.index((job, t)) + 1))
                    off = 0 if job[0] == "A" else (H_A + H_B) * HD + int(job[1]) * GRP * HD
                    probs = lambda b, h: pT[:, b, h, :]
                if n >= 1:
                    pe.wait_ge(o_read, nth(l, len(PVS), n))
                for h in range(GRP):
                    for b in range(t + 1):
                        last = pe.matmul(PVB[:, h * HD:(h + 1) * HD], probs(b, h), vs[:, b, off + h * HD:off + (h + 1) * HD],
                                         start=(b == 0), stop=(b == t))
                last.then_inc(pv_done, 1)

            for n in range(AHEAD // 2):
                sum_ada(n + 1, [0, 1], SB_).then_inc(modc_done, 1)
            with pe.Fori(0, L) as l:
                turn_h(l, 0)
                ffn(l, 0)
                pe.wait_ge(gate_ready, nth(l, 2 * NB, 2))
                turn_h(l, 1)
                wait_h(l, 1)
                for n in range(NC):
                    project(l, n)
                    if n < MID:
                        last = sum_ada(nth(l, ACC_L, AHEAD // 2 + NF + n + 1), [n % 2], PVB, n * CT)
                        if n == MID - 1:
                            last.then_inc(modc_done, 1)
                    if n in (3, 4, 5):
                        relevance(l, n - 3)
                    if n - 1 in NORMED:
                        sum_squares(l, n - 1)
                    if n in (7, 8):
                        attend(l, f"A{n - 7}")
                    if n in (9, 10):
                        stick(l, n - 9)
                    if n == 11:
                        turn_probs(l, "A0")
                    if n == 12:
                        values(l, "A0")
                cumulate(l)
                attend(l, "C00")
                turn_probs(l, "A1")
                values(l, "A1")
                attend(l, "C01")
                values(l, "B0")
                values(l, "B1")
                turn_probs(l, "C00")
                values(l, "C00")
                attend(l, "C10")
                turn_probs(l, "C01")
                values(l, "C01")
                attend(l, "C11")
                turn_probs(l, "C10")
                values(l, "C10")
                turn_probs(l, "C11")
                values(l, "C11")
                pe.wait_ge(zc_ready, nth(l, 3, 3))
                spread_gate(l, 1)
                turn_h(l, 3)
                wait_h(l, 3)
                pe.wait_ge(gate_ready, nth(l, 2 * NB, 4))
                for n, (k0, nk) in enumerate(OUT_CHUNKS):
                    slot = n % NSLOT
                    pe.wait_ge(split_done[slot], turn(l, U_OUT + n // NSLOT) + 2)
                    for k in range(nk):
                        kt = k0 + k
                        for t in range(TT):
                            tok = slice(t * P, (t + 1) * P)
                            for half in range(2):
                                w = slice(k * D + half * HALF, k * D + (half + 1) * HALF)
                                last = three(DB[2 * t + half][:, :], hhi[:, kt, tok], hlo[:, kt, tok], whi[slot][:, w], wlo[slot][:, w],
                                             kt == 0, kt == KT - 1)
                    last.then_inc(out_done, 1)
                turn_h(l, 2)
                ffn(l, 1)


_INS = ['x', 'c', 'w_ada', 'b_ada', 'norm_ffn1', 'w_gate1', 'w_up1', 'w_down1', 'norm_mix', 'w_in', 'qn_a', 'kn_a',
        'qn_c', 'kn_c', 'g_out', 'w_out', 'norm_ffn2', 'w_gate2', 'w_up2', 'w_down2']


def kernel(**inputs):
    import numpy as _np
    import concourse.bacc as _bacc
    from concourse import mybir as _mybir
    from concourse.bass_utils import run_bass_kernel_spmd as _run

    nc = _bacc.Bacc("TRN2", target_bir_lowering=False, num_devices=1)
    arrays, args = {}, []
    for name in _INS:
        a = _np.ascontiguousarray(inputs[name])
        arrays[f"in_{name}_dram"] = a
        args.append(nc.dram_tensor(f"in_{name}_dram", a.shape, _mybir.dt.from_np(a.dtype), kind="ExternalInput").ap())
    shape = inputs["x"].shape
    args.append(nc.dram_tensor("out_0_dram", shape, _mybir.dt.float32, kind="ExternalOutput").ap())
    build(nc, *args)
    r = _run(nc, [arrays], core_ids=[0])
    return r.results[0]["out_0_dram"]
```

```python
from contextlib import ExitStack

import numpy as np

import concourse.bass as bass
from concourse import mybir

F32 = mybir.dt.float32
F32R = mybir.dt.float32r
BF16 = mybir.dt.bfloat16
I32 = mybir.dt.int32
ALU = mybir.AluOpType
ACT = mybir.ActivationFunctionType
AX_X = mybir.AxisListType.X

P = 128
HD = 64
H_A, H_B, H_C, H_I = 4, 4, 8, 8
DILATIONS = ((128, 1), (512, 4), (2048, 16))
EPS = 1e-6
NEG = -1e30
TAKEN = -3e38
CW = 256
NSLOT = 3
N_MOD = 9
GRP = 4


def slopes():
    n = H_A + H_C
    every = np.exp2(np.float32(-8.0) * np.arange(1, n + 1, dtype=np.float32) / np.float32(n))
    return [float(s) for i, s in enumerate(every) if i % 3 == 2], [float(s) for i, s in enumerate(every) if i % 3 != 2]


def build(nc, x, c, w_ada, b_ada, norm_ffn1, w_gate1, w_up1, w_down1, norm_mix, w_in, qn_a, kn_a, qn_c, kn_c,
          g_out, w_out, norm_ffn2, w_gate2, w_up2, w_down2, out):
    _, S, D = x.shape
    L = w_in.shape[0]
    FF = w_gate1.shape[2]
    KT = D // P
    TT = S // P
    NF = FF // CW
    FT = FF // P
    HALF = 512
    TOPK = min(256, S // 4)
    assert D == 1024 and S == 256 and FF % CW == 0 and TT == 2 and TOPK % 8 == 0

    sizes = [H_A * HD] * 3 + [H_I * HD, HD, H_I] + [H_B * HD] * 3 + [H_C * HD] * 3
    at = dict(zip(("qa", "ka", "va", "qi", "ki", "wi", "qb", "kb", "vb", "qc", "kc", "vc"), np.cumsum([0] + sizes[:-1]).tolist()))
    CHUNKS = [("qi", 0), ("qi", 1), ("ki", 0), ("kc", 0), ("qc", 0), ("vc", 0), ("kb", 0), ("qb", 0),
              ("kc", 1), ("qc", 1), ("ka", 0), ("qa", 0), ("vb", 0), ("vc", 1), ("va", 0)]
    NC = len(CHUNKS)
    NORMED = [n for n, (k, _) in enumerate(CHUNKS) if k in ("ka", "qa", "kc", "qc")]
    GAIN = {"qa": 0, "ka": 1, "qc": 2, "kc": 3}
    OUT_CHUNKS = [(0, 1), (1, 1), (2, 1), (3, 1), (4, 2), (6, 2)]
    U_FFN = (0, NF + NC // NSLOT + len(OUT_CHUNKS) // NSLOT)
    U_IN = NF
    U_OUT = NF + NC // NSLOT
    U_LAYER = U_FFN[1] + NF
    ADA_L = N_MOD * D // CW
    AHEAD = 2 * D // CW
    MID = ADA_L - 3 * NF
    CT = CW // P
    assert MID == 3 and KT * N_MOD == ADA_L * CT
    ADA_PRE = AHEAD // 2
    ADA_TURNS = (NF + 2 + NF, NF + 1)

    wide = lambda w: w.rearrange("l (k p) n -> p (l k) n", p=P)
    v_gate, v_up, v_down = map(wide, (w_gate1, w_up1, w_down1))
    v_gate2, v_up2, v_down2 = map(wide, (w_gate2, w_up2, w_down2))
    v_in, v_out, v_ada = map(wide, (w_in, w_out, w_ada))
    x_v = x.rearrange("b (t p) d -> p (b t) d", p=P)
    out_v = out.rearrange("b (t p) d -> p (b t) d", p=P)

    ctx = ExitStack()
    with ctx:
        def sb(name, shape, dt=F32):
            return ctx.enter_context(nc.sbuf_tensor(name, shape, dt))

        def sem(name):
            return ctx.enter_context(nc.semaphore(name))

        raw = [sb(f"raw{k}", [P, 8 * CW]) for k in range(NSLOT)]
        whi = [sb(f"whi{k}", [P, 8 * CW], F32R) for k in range(NSLOT)]
        wlo = [sb(f"wlo{k}", [P, 8 * CW], F32R) for k in range(NSLOT)]
        ada = sb("ada", [P, 2, KT, CW])
        xs = sb("xs", [P, TT, D])
        xn = sb("xn", [P, TT, D])
        hTf = sb("hTf", [P, KT, S])
        hhi = sb("hhi", [P, KT, S], F32R)
        hlo = sb("hlo", [P, KT, S], F32R)
        gate = sb("gate", [P, D])
        qk1 = sb("qk1", [P, 4, S])
        qcT = sb("qcT", [P, 4, S])
        kcT = sb("kcT", [P, 4, S])
        sqr = sb("sqr", [P, 2, S])
        rqk = sb("rqk", [P, 2, S])
        selb = sb("selb", [P, TT, S])
        qbT = sb("qbT", [P, 2, S])
        kbT = sb("kbT", [P, 2, S])
        kiT = sb("kiT", [P, S])
        vs = sb("vs", [P, TT, D])
        wi = sb("wi", [P, TT, H_I])
        aliA = sb("aliA", [P, H_A, S])
        aliC = sb("aliC", [P, H_C, S])
        causal = sb("causal", [P, S])
        strictT = sb("strictT", [P, S], BF16)
        ident = sb("ident", [P, P])
        ones = sb("ones", [P, P])
        heads1 = sb("heads1", [P, P])
        upper = sb("upper", [P, P])
        zero16 = sb("zero16", [P, HALF], BF16)
        LG = [sb(f"LG{k}", [P, 4 * S]) for k in range(2)]
        pT = sb("pT", [P, TT, GRP, P])
        eb = sb("eb", [P, GRP * (S + P)])
        guhi = sb("guhi", [P, 2 * S], F32R)
        gulo = sb("gulo", [P, 2 * S], F32R)
        top8 = sb("top8", [P, 8])
        cT = sb("cT", [P, KT])
        acc = sb("acc", [P, MID, CW])
        modc = sb("modc", [P, (N_MOD + 2) * KT])
        biasL = sb("biasL", [P, N_MOD, KT])
        cols = sb("cols", [P, L, KT, 13])
        colL = sb("colL", [P, KT, 13])
        qkg = sb("qkg", [P, L, 4])
        qkgL = sb("qkgL", [P, 4])
        modA = sb("modA", [P, KT])
        modB = sb("modB", [P, KT])
        ss = sb("ss", [P, TT, 4])
        var = sb("var", [P, TT, 4])
        rs = sb("rs", [P, TT, 4])
        tn = sb("tn", [P, TT, 4])
        rstd = sb("rstd", [P, TT, 4])
        mx = sb("mx", [P, 6, GRP])
        sm = sb("sm", [P, 6, GRP])
        rsm = sb("rsm", [P, 6, GRP])
        eps = sb("eps", [P, 1])
        rows = vs[0:N_MOD + 4, :, :]
        score = acc
        silu = eb[:, 0:2 * S]
        guf = eb[:, 2 * S:4 * S]
        zf = hTf[:, :, :].rearrange("p k s -> p (k s)")
        z0 = zf[:, 0:GRP * S].rearrange("p (h s) -> p h s", h=GRP)
        z1 = zf[:, GRP * S:GRP * (S + P)].rearrange("p (h s) -> p h s", h=GRP)
        e0 = eb[:, 0:GRP * S].rearrange("p (h s) -> p h s", h=GRP)
        e1 = eb[:, GRP * S:GRP * (S + P)].rearrange("p (h s) -> p h s", h=GRP)
        disti = hTf[:, 0, :].bitcast(I32)
        dm4 = hTf[:, 1, :].bitcast(I32)
        dm16 = hTf[:, 2, :].bitcast(I32)
        strict_i = hTf[:, 3, :].bitcast(I32)
        upper_i = hTf[:, 4, 0:P].bitcast(I32)
        ident_i = hTf[:, 5, 0:P].bitcast(I32)
        distf = xn[:, 0, 0:S]
        ge0 = xn[:, 0, S:2 * S]
        tmpf = xn[:, 0, 2 * S:3 * S]
        maskC = xn[:, 0, 3 * S:4 * S]

        PS = [ctx.enter_context(nc.psum_tensor(f"bank{i}", [P, HALF], F32)) for i in range(8)]
        DB = PS[0:4]
        GB, UB0, UB1, SB_ = PS[4], PS[5], PS[6], PS[7]
        PROJ = [PS[0], PS[1], PS[7]]
        EVEN, ODD, SSB, TRB, PVB = PS[3], PS[4], PS[2], PS[5], PS[6]

        raw_full = [sem(f"raw_full{k}") for k in range(NSLOT)]
        hi_full = [sem(f"hi_full{k}") for k in range(NSLOT)]
        split_done = [sem(f"split_done{k}") for k in range(NSLOT)]
        ada_full = [sem(f"ada_full{k}") for k in range(2)]
        ada_used = [sem(f"ada_used{k}") for k in range(2)]
        acc_ready = sem("acc_ready")
        modc_done = sem("modc_done")
        diag_ready = sem("diag_ready")
        gate_done = sem("gate_done")
        x_in = sem("x_in")
        rows_in = sem("rows_in")
        gains_in = sem("gains_in")
        c_in = sem("c_in")
        iotas = sem("iotas")
        tables = sem("tables")
        silu_c = sem("silu_c")
        cols_done = sem("cols_done")
        x_out = sem("x_out")
        sumsq = sem("sumsq")
        var_ready = sem("var_ready")
        rs_ready = sem("rs_ready")
        xn_ready = sem("xn_ready")
        tp_done = sem("tp_done")
        hTf_ready = sem("hTf_ready")
        hhi_ready = sem("hhi_ready")
        h_ready = sem("h_ready")
        out_done = sem("out_done")
        gate_ready = sem("gate_ready")
        g_done = sem("g_done")
        silu_ready = sem("silu_ready")
        u_done = sem("u_done")
        gu_ready = sem("gu_ready")
        guhi_ready = sem("guhi_ready")
        gulo_ready = sem("gulo_ready")
        d_done = sem("d_done")
        x_ready = sem("x_ready")
        proj_done = sem("proj_done")
        proj_act = sem("proj_act")
        proj_dve = sem("proj_dve")
        sq_ready = sem("sq_ready")
        ssq_done = sem("ssq_done")
        rqk_ready = sem("rqk_ready")
        pair_done = sem("pair_done")
        rel_read = sem("rel_read")
        rel_used = sem("rel_used")
        pair_read = sem("pair_read")
        logits_ready = sem("logits_ready")
        exps_ready = sem("exps_ready")
        tr_done = sem("tr_done")
        pT_ready = sem("pT_ready")
        pv_done = sem("pv_done")
        o_read = sem("o_read")
        ln_ready = sem("ln_ready")
        log1m_ready = sem("log1m_ready")
        cum_done = sem("cum_done")
        zc_ready = sem("zc_ready")
        a_ready = sem("a_ready")

        block = ctx.enter_context(nc.Block())

        PAIRS = ["rel0", "rel1", "rel2", "C00", "C01", "Z0", "Z1", "C10", "C11", "A0", "A1"]
        SOFT = ["C00", "C01", "C10", "C11", "A0", "A1"]
        TRS = [(s, b) for s in SOFT for b in range(int(s[-1]) + 1)]
        PVS = ["C00", "C01", "C10", "C11", "B0", "B1", "A0", "A1"]
        PAIR_READS = PAIRS[3:]
        TPB = ((PS[4], PS[5]), (PS[6], PS[0]))
        GATES = ((PS[4], PS[5]), (PS[7], PS[2]), (PS[4], PS[5]))
        CUM = (PS[2], PS[5], PS[6])
        LATE = ("A1",)

        def in_pair(job):
            return (PS[0], PS[1]) if job in LATE else (EVEN, ODD)

        def width(job):
            return P * (int(job[-1]) + 1)

        def logits_of(job):
            return LG[SOFT.index(job) % 2][:, 0:GRP * width(job)].rearrange("p (h s) -> p h s", h=GRP)

        def chunk_cols(w, n=CW):
            return w[:, :].rearrange("p (k n) -> p k n", k=8)[:, :, 0:n]

        def at_cols(start, n):
            return slice(start, start + n) if isinstance(start, int) else bass.ds(start, n)

        def turn(l, n):
            return l * U_LAYER + n

        def copied(n):
            return sum(m not in NORMED for m in range(n + 1))

        def nth(l, per_layer, n):
            return l * per_layer + n

        def ada_turn(l, slot, n):
            return ADA_PRE + l * ADA_TURNS[slot] + n

        MODC_PRE = AHEAD // 2
        MODC_L = NF + 1 + NF
        ACC_L = NF + MID + NF

        NB = 3
        NN = 4 * TT
        NORM_AT = {0: 0, 1: 1, 3: 2, 2: 3}

        @block.sync
        def _(sp):
            sp.dma_start(cT[:, :], c.rearrange("b (k p) -> p (b k)", p=P), allow_slow_non_contiguous=True).then_inc(c_in, 16)
            sp.dma_start(xs[:, :, :], x_v).then_inc(x_in, 16)
            sp.dma_start(rows[0:N_MOD, :, :], b_ada.rearrange("l (m d) -> m l d", d=D)).then_inc(rows_in, 16)
            for n, g in enumerate((norm_ffn1, norm_mix, norm_ffn2, g_out)):
                sp.dma_start(rows[N_MOD + n:N_MOD + n + 1, :, :], g.rearrange("(a l) d -> a l d", a=1)).then_inc(rows_in, 16)
            for n, g in enumerate((qn_a, kn_a, qn_c, kn_c)):
                for half in range(2):
                    sp.dma_start(qkg[half * HD:half * HD + HD, :, n], g.rearrange("l p -> p l"),
                                 allow_slow_non_contiguous=True).then_inc(gains_in, 16)

            def fill(slot, use, dst, src, waited=False):
                if not waited:
                    sp.wait_ge(split_done[slot], use + 1)
                sp.dma_start(dst, src).then_inc(raw_full[slot], 16)

            def ffn(l, base, wg, wu, wd):
                with sp.Fori(0, NF) as i:
                    use, k0, f0, r0 = (sp.snap(v) for v in (turn(l, base) + i, l * KT, i * CW, l * FT + i * 2))
                    fill(0, use, chunk_cols(raw[0]), wg[:, bass.ds(k0, KT), bass.ds(f0, CW)])
                    fill(1, use, chunk_cols(raw[1]), wu[:, bass.ds(k0, KT), bass.ds(f0, CW)])
                    fill(2, use, raw[2][:, :].rearrange("p (k n) -> p k n", k=2), wd[:, bass.ds(r0, 2), :])

            QA = CHUNKS.index(("qa", 0))
            with sp.Fori(0, L) as l:
                ffn(l, U_FFN[0], v_gate, v_up, v_down)
                k_in = sp.snap(l * KT)
                for n, (kind, part) in enumerate(CHUNKS):
                    w = HD + H_I if kind == "ki" else CW
                    col = at[kind] + part * CW
                    if n == QA - 1:
                        for m in (QA - 1, QA):
                            sp.wait_ge(split_done[m % NSLOT], turn(l, U_IN + m // NSLOT) + 1)
                    fill(n % NSLOT, turn(l, U_IN + n // NSLOT), chunk_cols(raw[n % NSLOT], w),
                         v_in[:, bass.ds(k_in, KT), col:col + w], waited=n in (QA - 1, QA))
                for n, (k0, nk) in enumerate(OUT_CHUNKS):
                    fill(n % NSLOT, turn(l, U_OUT + n // NSLOT),
                         raw[n % NSLOT][:, 0:nk * D].rearrange("p (k n) -> p k n", k=nk), v_out[:, bass.ds(l * KT + k0, nk), :])
                ffn(l, U_FFN[1], v_gate2, v_up2, v_down2)
            for t in range(TT):
                sp.wait_ge(x_ready, NB * TT * L + t + 1)
                sp.dma_start(out_v[:, t, :], xs[:, t, :]).then_inc(x_out, 16)
            sp.wait_ge(x_out, 16 * TT)

        @block.gpsimd
        def _(pool):
            pool.iota(disti, pattern=[[-1, S]], base=P, channel_multiplier=1).then_inc(iotas, 1)
            pool.iota(strict_i, pattern=[[1, S]], base=0, channel_multiplier=-1).then_inc(iotas, 1)
            pool.iota(upper_i, pattern=[[-1, P]], base=0, channel_multiplier=1).then_inc(iotas, 1)

            def fill(slot, turn_, row, col):
                pool.wait_ge(ada_used[slot], turn_)
                pool.dma_start(ada[:, slot, :, :], v_ada[:, row, col]).then_inc(ada_full[slot], 16)

            for m in range(AHEAD):
                fill(m % 2, m // 2 + 1, slice(0, KT), slice(m * CW, (m + 1) * CW))
            with pool.Fori(0, L) as l:
                rows_l = pool.snap(l * KT)
                with pool.Fori(0, NF) as i:
                    for k in range(2):
                        fill(k, ada_turn(l, k, i + 1), bass.ds(rows_l, KT), bass.ds(i * (2 * CW) + (AHEAD + k) * CW, CW))
                for n in range(MID):
                    m = AHEAD + 2 * NF + n
                    fill(n % 2, ada_turn(l, n % 2, NF + n // 2 + 1), bass.ds(rows_l, KT), slice(m * CW, (m + 1) * CW))
                with pool.Fori(0, NF - AHEAD) as i:
                    fill(0, ada_turn(l, 0, NF + 2 + i + 1), bass.ds(rows_l, KT), bass.ds(i * CW + (ADA_L - (NF - AHEAD)) * CW, CW))
                rows_n = pool.snap((l + 1) % L * KT)
                with pool.Fori(0, AHEAD) as i:
                    fill(0, ada_turn(l, 0, NF + 2 + NF - AHEAD + i + 1), bass.ds(rows_n, KT), bass.ds(i * CW, CW))

        @block.scalar
        def _(act):
            act.wait_ge(c_in, 16)
            act.activation(cT[:, :], cT[:, :], ACT.Silu).then_inc(silu_c, 1)

            def split_hi(slot, use, pieces=None):
                act.wait_ge(raw_full[slot], (use + 1) * 16)
                if pieces is None:
                    pieces = [(whi[slot][:, :], raw[slot][:, :])]
                for dst, src in pieces:
                    last = act.activation(dst, src, ACT.Copy)
                last.then_inc(hi_full[slot], 1)

            def root(l, n, t, groups):
                act.wait_ge(var_ready, nth(l, NN, NORM_AT[n] * TT + t + 1))
                act.activation(rs[:, t, 0:groups], var[:, t, 0:groups], ACT.Ln)
                act.drain()
                act.activation(rs[:, t, 0:groups], rs[:, t, 0:groups], ACT.Exp, scale=-0.5).then_inc(rs_ready, 1)

            def boundary(l, n, x_done):
                for t in range(TT):
                    act.wait_ge(x_ready, x_done + t + 1)
                    act.activation(xn[:, t, :], xs[:, t, :], ACT.Square, accum_out=ss[:, t, 0:1]).then_inc(sumsq, 1)
                    root(l, n, t, 1)
                high_of_h(l, n)

            def copy_gate(l, n):
                act.wait_ge(gate_done, nth(l, NB, n + 1))
                for half in range(2):
                    act.activation(gate[:, half * HALF:(half + 1) * HALF], GATES[n][half][:, :], ACT.Copy,
                                   scale=1.0 if n == 1 else 0.5).then_inc(gate_ready, 1)

            def high_of_h(l, n):
                for t in range(TT):
                    act.wait_ge(hTf_ready, nth(l, NN, NORM_AT[n] * TT + t + 1))
                    act.activation(hhi[:, :, t * P:(t + 1) * P], hTf[:, :, t * P:(t + 1) * P], ACT.Copy).then_inc(hhi_ready, 1)

            def ffn_step(l, which, i, ahead):
                base = turn(l, U_FFN[which])
                n = nth(l, 2 * NF, which * NF) + i
                act.wait_ge(g_done, n + 1)
                act.activation(silu, GB[:, :], ACT.Silu).then_inc(silu_ready, 1)
                split_hi(2, base + i)
                for ft in range(2):
                    act.wait_ge(gu_ready, n * 2 + ft + 1)
                    act.activation(guhi[:, ft * S:(ft + 1) * S], guf[:, ft * S:(ft + 1) * S], ACT.Copy).then_inc(guhi_ready, 1)
                    if ahead:
                        split_hi(ft, base + i + 1)

            def ffn(l, which):
                with act.Fori(0, NF - 1) as i:
                    ffn_step(l, which, i, True)
                ffn_step(l, which, NF - 1, False)

            def mix_split(l, n):
                slot = n % NSLOT
                pieces = None
                if CHUNKS[n][0] == "ki":
                    r = chunk_cols(raw[slot])
                    w = chunk_cols(whi[slot])
                    pieces = [(w[:, :, 0:HD], r[:, :, 0:HD]), (w[:, :, HD:2 * HD], r[:, :, 0:HD]),
                              (w[:, :, P:P + H_I], r[:, :, HD:HD + H_I])]
                split_hi(slot, turn(l, U_IN + n // NSLOT), pieces)

            def evacuate(l, n):
                kind, part = CHUNKS[n]
                bank = PROJ[n % 3]
                act.wait_ge(proj_done, nth(l, NC, n + 1))
                if n in NORMED:
                    act.activation(sqr[:, :, :], bank[:, :].rearrange("p (a s) -> p a s", a=2), ACT.Square).then_inc(sq_ready, 1)
                    return
                both = bank[:, :].rearrange("p (a s) -> p a s", a=2)
                if kind == "qi":
                    last = act.activation(qk1[:, 2 * part:2 * part + 2, :], both, ACT.Copy)
                elif kind == "ki":
                    act.activation(kiT[:, :], bank[:, 0:S], ACT.Copy)
                    last = act.activation(wi[:, :, :], bank[:, S:S + TT * H_I].rearrange("p (t h) -> p t h", t=TT), ACT.Copy)
                elif kind in ("qb", "kb"):
                    last = act.activation((qbT if kind == "qb" else kbT)[:, :, :], both, ACT.Copy)
                else:
                    off = {"va": 0, "vb": H_A * HD, "vc": (H_A + H_B) * HD}[kind] + part * CW
                    last = act.activation(vs[:, :, off:off + CW], both, ACT.Copy)
                last.then_inc(proj_act, 1)

            def inv_rms(l, n):
                j = NORMED.index(n)
                act.wait_ge(ssq_done, nth(l, len(NORMED), j + 1))
                if j >= 1:
                    act.wait_ge(proj_dve, nth(l, len(NORMED), j))
                act.activation(rqk[:, :, :], SSB[:, :].rearrange("p (a s) -> p a s", a=2), ACT.Ln, scale=1.0 / HD, bias=eps[:, :])
                act.drain()
                act.activation(rqk[:, :, :], rqk[:, :, :], ACT.Exp, scale=-0.5).then_inc(rqk_ready, 1)

            def rel_relu(l, j):
                act.wait_ge(pair_done, nth(l, len(PAIRS), j + 1))
                if j >= 2:
                    act.wait_ge(rel_used, nth(l, 3, j - 1))
                for odd in range(2):
                    last = act.activation(LG[j % 2][:, odd * HALF:(odd + 1) * HALF], (EVEN, ODD)[odd][:, :], ACT.Relu)
                last.then_inc(rel_read, 1)

            def exps(l, job):
                j = SOFT.index(job)
                act.wait_ge(logits_ready, nth(l, len(SOFT), j + 1))
                lg = logits_of(job)
                for h in range(GRP):
                    last = act.activation(lg[:, h, :], lg[:, h, :], ACT.Exp, bias=mx[:, j, h:h + 1], accum_out=sm[:, j, h:h + 1])
                last.then_inc(exps_ready, 1)

            def copy_pT(l, job, *blocks):
                for b in blocks:
                    n = TRS.index((job, b))
                    act.wait_ge(tr_done, nth(l, len(TRS), n + 1))
                    act.activation(pT[:, b, :, :], TRB[:, :].rearrange("p (h t) -> p h t", h=GRP), ACT.Copy).then_inc(pT_ready, 1)

            def softplus_log(l, st):
                z, e = ((z0, e0), (z1, e1))[st]
                act.wait_ge(pair_read, nth(l, 8, PAIR_READS.index(f"Z{st}") + 1))
                act.activation(e, z, ACT.Abs)
                act.drain()
                act.activation(e, e, ACT.Exp, scale=-1.0)
                act.drain()
                act.activation(e, e, ACT.Ln, bias=1.0).then_inc(ln_ready, 1)

            def stick_exps(l):
                for j in range(3):
                    act.wait_ge(zc_ready, nth(l, 3, j + 1))
                    part = z1 if j == 2 else z0[:, 2 * j:2 * j + 2, :]
                    act.activation(part, part, ACT.Exp).then_inc(a_ready, 1)

            act.wait_ge(tables, 2)
            act.wait_ge(x_in, 16)
            with act.Fori(0, L) as l:
                act.preload_act_table_set("natural_log_exp_and_others")
                boundary(l, 0, nth(l, NB * TT, 0))
                act.preload_act_table(ACT.Silu)
                for k in range(2):
                    split_hi(k, turn(l, U_FFN[0]))
                ffn(l, 0)
                copy_gate(l, 0)
                act.preload_act_table_set("natural_log_exp_and_others")
                boundary(l, 1, nth(l, NB * TT, TT))
                mix_split(l, 0)
                mix_split(l, 1)
                for n in range(NC + 1):
                    if n >= 2 and n - 2 in NORMED:
                        inv_rms(l, n - 2)
                    if n >= 1:
                        evacuate(l, n - 1)
                    if n + 2 < NC:
                        mix_split(l, n + 2)
                    if n in (4, 5, 6):
                        rel_relu(l, n - 4)
                    if n == 1:
                        copy_gate(l, 1)
                    if n == 8:
                        exps(l, "C00")
                    if n == 9:
                        exps(l, "C01")
                    if n == 10:
                        copy_pT(l, "C00", 0)
                        softplus_log(l, 0)
                    if n == 11:
                        copy_pT(l, "C01", 0)
                        softplus_log(l, 1)
                    if n == 12:
                        copy_pT(l, "C01", 1)
                    if n == 13:
                        exps(l, "C10")
                    if n == 14:
                        exps(l, "C11")
                        stick_exps(l)
                exps(l, "A0")
                copy_pT(l, "C10", 0)
                for k in range(NSLOT):
                    split_hi(k, turn(l, U_OUT), [(whi[k][:, 0:D], raw[k][:, 0:D])])
                copy_pT(l, "C11", 0, 1)
                exps(l, "A1")
                copy_pT(l, "A0", 0)
                copy_pT(l, "A1", 0, 1)
                for t in range(TT):
                    act.wait_ge(o_read, nth(l, len(PVS), len(PVS) - 1 + t))
                    for g, (a, b) in enumerate(((0, 256), (256, 512), (512, 1024))):
                        last = act.activation(eb[:, a:b], xn[:, t, a:b], ACT.Square, accum_out=ss[:, t, g:g + 1])
                    last.then_inc(sumsq, 1)
                    root(l, 3, t, 3)
                high_of_h(l, 3)
                for n in range(NSLOT, len(OUT_CHUNKS)):
                    k = n % NSLOT
                    nk = OUT_CHUNKS[n][1]
                    act.wait_ge(out_done, nth(l, len(OUT_CHUNKS), n - NSLOT + 1))
                    split_hi(k, turn(l, U_OUT + 1), [(whi[k][:, 0:nk * D], raw[k][:, 0:nk * D])])
                boundary(l, 2, nth(l, NB * TT, 2 * TT))
                act.preload_act_table(ACT.Silu)
                for k in range(2):
                    split_hi(k, turn(l, U_FFN[1]))
                ffn(l, 1)
                copy_gate(l, 2)

        @block.vector
        def _(dve):
            for k in range(NSLOT):
                dve.sem_inc(split_done[k], 1)
            for k in range(2):
                dve.sem_inc(ada_used[k], 1)
            dve.memset(zero16[:, :], 0.0)
            dve.memset(ones[:, :], 1.0)
            dve.memset(heads1[:, :], 0.0)
            dve.memset(eps[:, :], EPS)
            dve.drain()
            for k in range(2):
                dve.memset(heads1[k * HD:(k + 1) * HD, k * HD:(k + 1) * HD], 1.0)
            dve.wait_ge(iotas, 3)
            dve.tensor_scalar(ident[:, :], upper_i, 0.0, None, ALU.is_equal)
            dve.tensor_scalar(upper[:, :], upper_i, 0.0, None, ALU.is_ge).then_inc(tables, 1)
            dve.tensor_scalar(strictT[:, :], strict_i, 0.0, NEG, ALU.is_le, ALU.mult)
            dve.tensor_scalar(dm4, disti, DILATIONS[1][1] - 1, None, ALU.bitwise_and)
            dve.tensor_scalar(dm16, disti, DILATIONS[2][1] - 1, None, ALU.bitwise_and)
            dve.tensor_copy(distf, disti)
            dve.drain()
            dve.tensor_scalar(ge0, distf, 0.0, None, ALU.is_ge)
            dve.tensor_scalar(causal[:, :], distf, 0.0, NEG, ALU.is_lt, ALU.mult)
            dve.tensor_scalar(tmpf, dm4, 0.0, None, ALU.is_equal)
            dve.tensor_scalar(maskC, dm16, 0.0, None, ALU.is_equal)
            dve.drain()
            dve.tensor_tensor(tmpf, tmpf, maskC, ALU.add)
            dve.drain()
            dve.scalar_tensor_tensor(tmpf, distf, float(DILATIONS[0][0]), tmpf, ALU.is_le, ALU.add)
            dve.drain()
            dve.tensor_tensor(tmpf, tmpf, ge0, ALU.mult)
            dve.drain()
            dve.tensor_scalar(maskC, tmpf, 0.0, NEG, ALU.is_equal, ALU.mult)
            for m in (2, 3):
                dve.drain()
                dve.tensor_scalar(ge0, tmpf, float(m), float(np.log(m)), ALU.is_equal, ALU.mult)
                dve.drain()
                dve.tensor_tensor(maskC, maskC, ge0, ALU.add)
            dve.drain()
            s_a, s_c = slopes()
            for h in range(H_A):
                dve.scalar_tensor_tensor(aliA[:, h, :], distf, -s_a[h], causal[:, :], ALU.mult, ALU.add)
            for h in range(H_C):
                dve.scalar_tensor_tensor(aliC[:, h, :], distf, -s_c[h], maskC, ALU.mult, ALU.add)
            dve.wait_ge(cols_done, 1)
            dve.tensor_copy(cols[:, :, :, :], PS[0][:, 0:L * KT * 13].rearrange("p (l k m) -> p l k m", l=L, k=KT))
            dve.wait_ge(x_in, 16)
            dve.sem_inc(x_ready, TT)
            dve.wait_ge(gains_in, 8 * 16)
            dve.drain().then_inc(tables, 1)

            def weigh_ada(turns, slots, to=None):
                for slot, n in zip(slots, turns):
                    dve.wait_ge(ada_full[slot], n * 16)
                a, b = slots[0], slots[-1] + 1
                to = slots[0] if to is None else to
                sums = acc[:, to:to + b - a, :]
                for k in range(KT):
                    if k == 0:
                        dve.tensor_scalar(sums, ada[:, a:b, k, :], cT[:, 0:1], None, ALU.mult)
                    else:
                        last = dve.scalar_tensor_tensor(sums, ada[:, a:b, k, :], cT[:, k:k + 1], sums, ALU.mult, ALU.add)
                    if k < KT - 1:
                        dve.drain()
                last.then_inc(acc_ready, 1)
                for slot in slots:
                    dve.drain().then_inc(ada_used[slot], 1)

            def read_modc(done, dst, bank):
                dve.wait_ge(modc_done, done)
                dve.tensor_copy(dst, bank)

            def diagonal(n):
                off = (3 * n + 2) * KT
                dve.drain()
                dve.tensor_tensor(modc[:, off:off + KT], modc[:, off:off + KT], biasL[:, 3 * n + 2, :], ALU.add)
                dve.drain()
                for k in range(KT):
                    last = dve.tensor_scalar(gate[:, k * P:(k + 1) * P], ident[:, :], modc[:, off + k:off + k + 1], None, ALU.mult)
                last.then_inc(diag_ready, 1)

            def split_lo(slot, use, pieces=None):
                dve.wait_ge(hi_full[slot], use + 1)
                if pieces is None:
                    pieces = [(wlo[slot][:, :], raw[slot][:, :], whi[slot][:, :])]
                for dst, src, hi in pieces:
                    last = dve.tensor_tensor(dst, src, hi.bitcast(F32), ALU.subtract)
                last.then_inc(split_done[slot], 1)

            def refine(l, n, t, groups, counts):
                dve.wait_ge(sumsq, nth(l, NN, NORM_AT[n] * TT + t + 1))
                if len(set(counts)) == 1:
                    dve.tensor_scalar(var[:, t, 0:groups], ss[:, t, 0:groups], 1.0 / counts[0], EPS, ALU.mult, ALU.add).then_inc(var_ready, 1)
                else:
                    for g, m in enumerate(counts):
                        last = dve.tensor_scalar(var[:, t, g:g + 1], ss[:, t, g:g + 1], 1.0 / m, EPS, ALU.mult, ALU.add)
                    last.then_inc(var_ready, 1)
                dve.wait_ge(rs_ready, nth(l, NN, NORM_AT[n] * TT + t + 1))
                dve.tensor_tensor(tn[:, t, 0:groups], rs[:, t, 0:groups], rs[:, t, 0:groups], ALU.mult)
                dve.drain()
                dve.tensor_tensor(tn[:, t, 0:groups], tn[:, t, 0:groups], var[:, t, 0:groups], ALU.mult)
                dve.drain()
                dve.tensor_scalar(tn[:, t, 0:groups], tn[:, t, 0:groups], -0.5, 1.5, ALU.mult, ALU.add)
                dve.drain()
                dve.tensor_tensor(rstd[:, t, 0:groups], tn[:, t, 0:groups], rs[:, t, 0:groups], ALU.mult)
                dve.drain()

            def transposed(l, n, gain, shift):
                for t in range(TT):
                    for half in range(2):
                        dve.wait_ge(tp_done, nth(l, 4 * 2 * TT, (NORM_AT[n] * TT + t) * 2 + half + 1))
                        bank = TPB[t][half]
                        for k in range(4):
                            kk = half * 4 + k
                            last = dve.tensor_scalar(hTf[:, kk, t * P:(t + 1) * P], bank[:, k * P:(k + 1) * P], gain[:, kk:kk + 1],
                                                     None if shift is None else shift[:, kk:kk + 1], ALU.mult,
                                                     **({} if shift is None else {"op1": ALU.add}))
                    last.then_inc(hTf_ready, 1)
                for t in range(TT):
                    dve.wait_ge(hhi_ready, nth(l, NN, NORM_AT[n] * TT + t + 1))
                    tok = slice(t * P, (t + 1) * P)
                    dve.tensor_tensor(hlo[:, :, tok], hTf[:, :, tok], hhi[:, :, tok].bitcast(F32), ALU.subtract).then_inc(h_ready, 1)

            def boundary(l, n):
                for t in range(TT):
                    refine(l, n, t, 1, [D])
                    dve.tensor_scalar(xn[:, t, :], xs[:, t, :], rstd[:, t, 0:1], None, ALU.mult).then_inc(xn_ready, 1)
                off = 3 * n * KT
                dve.tensor_tensor(modB[:, :], modc[:, off:off + KT], biasL[:, 3 * n, :], ALU.add)
                dve.tensor_tensor(modA[:, :], modc[:, off + KT:off + 2 * KT], biasL[:, 3 * n + 1, :], ALU.add)
                dve.drain()
                dve.scalar_tensor_tensor(modA[:, :], modA[:, :], 1.0, colL[:, :, N_MOD + n], ALU.add, ALU.mult)
                dve.drain()
                transposed(l, n, modA, modB)

            def residual(l, n):
                for t in range(TT):
                    if t == 0:
                        dve.wait_ge(gate_ready, nth(l, 2 * NB, 2 * n + 2))
                        if n == 1:
                            dve.wait_ge(out_done, nth(l, len(OUT_CHUNKS), len(OUT_CHUNKS)))
                        else:
                            dve.wait_ge(d_done, nth(l, 2, n // 2 + 1))
                    for half in range(2):
                        cut = slice(half * HALF, (half + 1) * HALF)
                        dve.tensor_tensor(xn[:, t, cut], DB[2 * t + half][:, :], gate[:, cut], ALU.mult)
                    dve.drain()
                    dve.tensor_tensor(xs[:, t, :], xs[:, t, :], xn[:, t, :], ALU.add).then_inc(x_ready, 1)

            def ffn_step(l, which, i, ahead):
                base = turn(l, U_FFN[which])
                n = nth(l, 2 * NF, which * NF) + i
                if which == 0:
                    weigh_ada([ada_turn(l, k, i + 1) for k in range(2)], [0, 1])
                else:
                    weigh_ada([ada_turn(l, 0, NF + 2 + i + 1)], [0])
                split_lo(2, base + i)
                dve.wait_ge(silu_ready, n + 1)
                for ft in range(2):
                    cut = slice(ft * S, (ft + 1) * S)
                    dve.wait_ge(u_done, n * 2 + ft + 1)
                    dve.tensor_tensor(guf[:, cut], silu[:, cut], (UB0, UB1)[ft][:, 0:S], ALU.mult).then_inc(gu_ready, 1)
                    dve.wait_ge(guhi_ready, n * 2 + ft + 1)
                    dve.tensor_tensor(gulo[:, cut], guf[:, cut], guhi[:, cut].bitcast(F32), ALU.subtract).then_inc(gulo_ready, 1)
                if which == 0:
                    read_modc(MODC_PRE + nth(l, MODC_L, 1) + i, modc[:, at_cols(AHEAD * CT + i * (2 * CT), 2 * CT)], SB_[:, 0:2 * CT])
                else:
                    read_modc(MODC_PRE + nth(l, MODC_L, NF + 2) + i, modc[:, at_cols((AHEAD + 2 * NF + MID) * CT + i * CT, CT)], SB_[:, 0:CT])
                if ahead:
                    for k in range(2):
                        split_lo(k, base + i + 1)

            def ffn(l, which):
                with dve.Fori(0, NF - 1) as i:
                    ffn_step(l, which, i, True)
                ffn_step(l, which, NF - 1, False)
                diagonal(2 * which)

            def mix_split(l, n):
                slot = n % NSLOT
                pieces = None
                if CHUNKS[n][0] == "ki":
                    r, w, v = chunk_cols(raw[slot]), chunk_cols(whi[slot]), chunk_cols(wlo[slot])
                    pieces = [(v[:, :, 0:HD], r[:, :, 0:HD], w[:, :, 0:HD]), (v[:, :, HD:2 * HD], r[:, :, 0:HD], w[:, :, HD:2 * HD]),
                              (v[:, :, P:P + H_I], r[:, :, HD:HD + H_I], w[:, :, P:P + H_I])]
                split_lo(slot, turn(l, U_IN + n // NSLOT), pieces)

            def head_norm(l, n):
                kind, part = CHUNKS[n]
                j = NORMED.index(n)
                dve.wait_ge(rqk_ready, nth(l, len(NORMED), j + 1))
                dst = {"qa": qk1[:, 0:2, :], "ka": qk1[:, 2:4, :], "qc": qcT[:, 2 * part:2 * part + 2, :],
                       "kc": kcT[:, 2 * part:2 * part + 2, :]}[kind]
                both = lambda a: a.rearrange("p (a s) -> p a s", a=2)
                dve.scalar_tensor_tensor(dst, both(PROJ[n % 3][:, :]), qkgL[:, GAIN[kind]:GAIN[kind] + 1], rqk[:, :, :],
                                         ALU.mult, ALU.mult).then_inc(proj_dve, 1)

            def weigh(l, j):
                dve.wait_ge(rel_read, nth(l, 3, j + 1))
                t = 0 if j == 0 else 1
                w = P * (t + 1)
                n_heads = 8 if j == 0 else 4
                sc = score[:, t, 0:w]
                for h in range(n_heads):
                    head = h + (4 if j == 2 else 0)
                    src = LG[j % 2][:, (h % 2) * HALF + (h // 2) * w:(h % 2) * HALF + (h // 2 + 1) * w]
                    if head == 0:
                        last = dve.tensor_scalar(sc, src, wi[:, t, 0:1], None, ALU.mult)
                    else:
                        last = dve.scalar_tensor_tensor(sc, src, wi[:, t, head:head + 1], sc, ALU.mult, ALU.add)
                    if h == n_heads - 1:
                        last.then_inc(rel_used, 1)
                    dve.drain()
                if j != 1:
                    dve.scalar_tensor_tensor(sc, sc, HD ** -0.5 * H_I ** -0.5, causal[:, S - w:S], ALU.mult, ALU.add)
                    dve.drain()

            def take_top(t, rounds):
                sc = score[:, t, 0:P * (t + 1)]
                for _ in range(rounds):
                    dve.max(top8[:, :], sc)
                    dve.drain()
                    dve.match_replace(sc, top8[:, :], sc, TAKEN)
                    dve.drain()

            def select(t):
                w = P * (t + 1)
                dve.tensor_scalar(selb[:, t, 0:w], score[:, t, 0:w], TAKEN, NEG, ALU.not_equal, ALU.mult)
                dve.drain()

            def logits(l, job):
                j = SOFT.index(job)
                w = width(job)
                lg = logits_of(job)
                even, odd = in_pair(job)
                bias = aliA if job[0] == "A" else aliC[:, GRP * int(job[1]):GRP * (int(job[1]) + 1), :]
                dve.wait_ge(pair_done, nth(l, len(PAIRS), PAIRS.index(job) + 1))
                if j >= 2:
                    dve.wait_ge(tr_done, nth(l, len(TRS), TRS.index((SOFT[j - 2], int(SOFT[j - 2][-1]))) + 1))
                for odd_, bank in enumerate((even, odd)):
                    last = dve.scalar_tensor_tensor(lg[:, odd_::2, :], bank[:, 0:2 * w].rearrange("p (h s) -> p h s", h=2), HD ** -0.5,
                                                    bias[:, odd_::2, S - w:S], ALU.mult, ALU.add)
                last.then_inc(pair_read, 1)
                dve.drain()
                if job[0] == "A":
                    t = int(job[-1])
                    dve.tensor_tensor(lg, lg, selb[:, t:t + 1, 0:w].to_broadcast([P, GRP, w]), ALU.add)
                    dve.drain()
                dve.tensor_reduce(mx[:, j, :], lg, AX_X, ALU.max)
                dve.drain()
                dve.tensor_scalar(mx[:, j, :], mx[:, j, :], -1.0, None, ALU.mult).then_inc(logits_ready, 1)

            def read_out(l, job):
                t = int(job[-1])
                off = {"A": 0, "B": H_A * HD}.get(job[0], (H_A + H_B) * HD + (int(job[1]) * GRP * HD if job[0] == "C" else 0))
                if job[0] != "B":
                    j = SOFT.index(job)
                    dve.wait_ge(exps_ready, nth(l, len(SOFT), j + 1))
                    dve.reciprocal(rsm[:, j, :], sm[:, j, :])
                    dve.drain()
                dve.wait_ge(pv_done, nth(l, len(PVS), PVS.index(job) + 1))
                dst = xn[:, t, off:off + GRP * HD]
                src = PVB[:, 0:GRP * HD]
                if job[0] == "B":
                    dve.tensor_copy(dst, src).then_inc(o_read, 1)
                else:
                    dve.tensor_tensor(dst.rearrange("p (h d) -> p h d", h=GRP), src.rearrange("p (h d) -> p h d", h=GRP),
                                      rsm[:, j, :].unsqueeze(2).to_broadcast([P, GRP, HD]), ALU.mult).then_inc(o_read, 1)

            def stick_logits(l, st):
                z = (z0, z1)[st]
                w = S - st * P
                dve.wait_ge(pair_done, nth(l, len(PAIRS), PAIRS.index(f"Z{st}") + 1))
                for odd_, bank in enumerate((EVEN, ODD)):
                    last = dve.scalar_tensor_tensor(z[:, odd_::2, :], bank[:, 0:2 * w].rearrange("p (h s) -> p h s", h=2), HD ** -0.5,
                                                    strictT[:, 0:w].unsqueeze(1).to_broadcast([P, 2, w]), ALU.mult, ALU.add)
                last.then_inc(pair_read, 1)

            def softplus(l, st):
                z, e = ((z0, e0), (z1, e1))[st]
                dve.wait_ge(ln_ready, nth(l, 2, st + 1))
                dve.scalar_tensor_tensor(e, z, 0.0, e, ALU.max, ALU.add).then_inc(log1m_ready, 1)

            def minus_cum(l):
                for j in range(3):
                    part = z1 if j == 2 else z0[:, 2 * j:2 * j + 2, :]
                    dve.wait_ge(cum_done, nth(l, 3, j + 1))
                    dve.tensor_tensor(part, part, CUM[j][:, :].rearrange("p (h s) -> p h s", h=4 if j == 2 else 2), ALU.subtract).then_inc(zc_ready, 1)

            dve.wait_ge(silu_c, 1)
            for n in range(AHEAD // 2):
                weigh_ada([n + 1, n + 1], [0, 1])
                read_modc(n + 1, modc[:, N_MOD * KT + 2 * CT * n:N_MOD * KT + 2 * CT * (n + 1)], SB_[:, 0:2 * CT])
                dve.drain()
            with dve.Fori(0, L) as l:
                dve.tensor_copy(colL[:, :, :], cols[:, bass.ds(l, 1), :, :].rearrange("p a k m -> p (a k) m"))
                dve.tensor_copy(modc[:, 0:2 * KT], modc[:, N_MOD * KT:(N_MOD + 2) * KT])
                dve.tensor_copy(biasL[:, :, :], cols[:, bass.ds(l, 1), :, 0:N_MOD].rearrange("p a k m -> p m (a k)"))
                dve.tensor_copy(qkgL[:, :], qkg[:, bass.ds(l, 1), :].rearrange("p a k -> p (a k)"))
                dve.drain()
                boundary(l, 0)
                for k in range(2):
                    split_lo(k, turn(l, U_FFN[0]))
                ffn(l, 0)
                residual(l, 0)
                boundary(l, 1)
                mix_split(l, 0)
                mix_split(l, 1)
                for n in range(NC + 1):
                    if n >= 2 and n - 2 in NORMED:
                        head_norm(l, n - 2)
                    if n + 2 < NC:
                        mix_split(l, n + 2)
                    if n == 0:
                        diagonal(1)
                    if n == 4:
                        weigh(l, 0)
                        take_top(0, TOPK // 16)
                    if n == 5:
                        weigh(l, 1)
                        take_top(0, TOPK // 16)
                        select(0)
                    if n == 6:
                        weigh(l, 2)
                        take_top(1, TOPK // 64)
                    if n == 7:
                        logits(l, "C00")
                        take_top(1, TOPK // 32)
                    if n == 8:
                        logits(l, "C01")
                    if n == 9:
                        stick_logits(l, 0)
                        take_top(1, TOPK // 32)
                    if n == 10:
                        stick_logits(l, 1)
                        take_top(1, TOPK // 64)
                    if n == 11:
                        read_out(l, "C00")
                        softplus(l, 0)
                        take_top(1, TOPK // 32)
                        select(1)
                    if n == 12:
                        softplus(l, 1)
                        logits(l, "C10")
                    if n == 13:
                        read_out(l, "C01")
                        logits(l, "C11")
                    if n == 14:
                        minus_cum(l)
                        logits(l, "A0")
                read_out(l, "C10")
                logits(l, "A1")
                read_out(l, "C11")
                read_out(l, "B0")
                read_out(l, "B1")
                read_out(l, "A0")
                for k in range(NSLOT):
                    split_lo(k, turn(l, U_OUT), [(wlo[k][:, 0:D], raw[k][:, 0:D], whi[k][:, 0:D])])
                read_out(l, "A1")
                for t in range(TT):
                    refine(l, 3, t, 3, [H_A * HD, H_B * HD, H_C * HD])
                    for g, (a, b) in enumerate(((0, 256), (256, 512), (512, 1024))):
                        last = dve.tensor_scalar(xn[:, t, a:b], xn[:, t, a:b], rstd[:, t, g:g + 1], None, ALU.mult)
                    last.then_inc(xn_ready, 1)
                transposed(l, 3, colL[:, :, 12], None)
                for n in range(NSLOT, len(OUT_CHUNKS)):
                    k = n % NSLOT
                    nk = OUT_CHUNKS[n][1]
                    split_lo(k, turn(l, U_OUT + 1), [(wlo[k][:, 0:nk * D], raw[k][:, 0:nk * D], whi[k][:, 0:nk * D])])
                    m = n - NSLOT
                    weigh_ada([ada_turn(l, m % 2, NF + m // 2 + 1)], [m % 2], m)
                off = (AHEAD + 2 * NF) * CT
                read_modc(MODC_PRE + nth(l, MODC_L, NF + 1), modc[:, off:off + MID * CT], PVB[:, 0:MID * CT])
                residual(l, 1)
                boundary(l, 2)
                for k in range(2):
                    split_lo(k, turn(l, U_FFN[1]))
                ffn(l, 1)
                residual(l, 2)

        @block.tensor
        def _(pe):
            pe.wait_ge(tables, 1)
            pe.wait_ge(rows_in, 5 * 16)
            for l in range(L):
                for k in range(KT):
                    o = (l * KT + k) * 13
                    last = pe.transpose(PS[0][:, o:o + 13], rows[:, l, k * P:(k + 1) * P], ident[0:13, 0:13])
            last.then_inc(cols_done, 1)

            def three(ps, l_hi, l_lo, r_hi, r_lo, first, last):
                pe.matmul(ps, l_hi, r_hi, start=first, stop=False)
                pe.matmul(ps, l_hi, r_lo, start=False, stop=False)
                return pe.matmul(ps, l_lo, r_hi, start=False, stop=last)

            def sum_ada(ready, slots, bank, at_=0):
                pe.wait_ge(acc_ready, ready)
                for slot in slots:
                    for j in range(CT):
                        last = pe.matmul(bank[:, at_:at_ + 1], acc[:, slot, j * P:(j + 1) * P], ones[:, 0:1], start=True, stop=True)
                        at_ += 1
                return last

            def spread_gate(l, n):
                pe.wait_ge(diag_ready, nth(l, NB, n + 1))
                for half in range(2):
                    last = pe.matmul(GATES[n][half][:, :], ones[:, :], gate[:, half * HALF:(half + 1) * HALF], start=True, stop=True)
                last.then_inc(gate_done, 1)

            def turn_h(l, n):
                for t in range(TT):
                    pe.wait_ge(xn_ready, nth(l, NN, NORM_AT[n] * TT + t + 1))
                    for half in range(2):
                        for k in range(4):
                            kk = half * 4 + k
                            last = pe.transpose(TPB[t][half][:, k * P:(k + 1) * P], xn[:, t, kk * P:(kk + 1) * P], ident[:, :])
                        last.then_inc(tp_done, 1)

            def wait_h(l, n):
                pe.wait_ge(h_ready, nth(l, NN, (NORM_AT[n] + 1) * TT))

            def ffn(l, which):
                wait_h(l, 2 * which)
                for b in range(4):
                    pe.matmul(DB[b][:, :], zero16[:, 0:P], zero16[:, :], start=True, stop=False)
                with pe.Fori(0, NF) as i:
                    use = turn(l, U_FFN[which]) + i
                    n = nth(l, 2 * NF, which * NF) + i
                    pe.wait_ge(split_done[0], use + 2)
                    wh, wl = chunk_cols(whi[0]), chunk_cols(wlo[0])
                    for ft in range(2):
                        for k in range(KT):
                            last = three(GB[:, ft * S:(ft + 1) * S], wh[:, k, ft * P:(ft + 1) * P], wl[:, k, ft * P:(ft + 1) * P],
                                         hhi[:, k, :], hlo[:, k, :], k == 0, k == KT - 1)
                    last.then_inc(g_done, 1)
                    pe.wait_ge(split_done[1], use + 2)
                    wh, wl = chunk_cols(whi[1]), chunk_cols(wlo[1])
                    for ft in range(2):
                        for k in range(KT):
                            last = three((UB0, UB1)[ft][:, 0:S], wh[:, k, ft * P:(ft + 1) * P], wl[:, k, ft * P:(ft + 1) * P],
                                         hhi[:, k, :], hlo[:, k, :], k == 0, k == KT - 1)
                        last.then_inc(u_done, 1)
                    if which == 0:
                        sum_ada(nth(l, ACC_L, AHEAD // 2 + 1) + i, [0, 1], SB_).then_inc(modc_done, 1)
                    else:
                        sum_ada(nth(l, ACC_L, AHEAD // 2 + NF + MID + 1) + i, [0], SB_).then_inc(modc_done, 1)
                    pe.wait_ge(split_done[2], use + 2)
                    for ft in range(2):
                        pe.wait_ge(gulo_ready, n * 2 + ft + 1)
                        for t in range(TT):
                            tok = slice(ft * S + t * P, ft * S + (t + 1) * P)
                            for half in range(2):
                                w = slice(ft * D + half * HALF, ft * D + (half + 1) * HALF)
                                last = three(DB[2 * t + half][:, :], guhi[:, tok], gulo[:, tok], whi[2][:, w], wlo[2][:, w], False, False)
                for b in range(4):
                    last = pe.matmul(DB[b][:, :], zero16[:, 0:P], zero16[:, :], start=False, stop=True)
                last.then_inc(d_done, 1)
                spread_gate(l, 2 * which)

            def project(l, n):
                kind, part = CHUNKS[n]
                slot = n % NSLOT
                bank = PROJ[n % 3]
                pe.wait_ge(split_done[slot], turn(l, U_IN + n // NSLOT) + 2)
                if n >= 3:
                    if n - 3 in NORMED:
                        pe.wait_ge(proj_dve, nth(l, len(NORMED), NORMED.index(n - 3) + 1))
                    else:
                        pe.wait_ge(proj_act, nth(l, NC - len(NORMED), copied(n - 3)))
                elif n == 2:
                    pe.wait_ge(gate_ready, nth(l, 2 * NB, 4))
                wh, wl = chunk_cols(whi[slot]), chunk_cols(wlo[slot])
                if kind[0] == "v":
                    for t in range(TT):
                        tok = slice(t * P, (t + 1) * P)
                        for k in range(KT):
                            last = three(bank[:, t * CW:(t + 1) * CW], hhi[:, k, tok], hlo[:, k, tok], wh[:, k, :], wl[:, k, :], k == 0, k == KT - 1)
                else:
                    for ct in range(1 if kind == "ki" else 2):
                        for k in range(KT):
                            cut = slice(ct * P, (ct + 1) * P)
                            last = three(bank[:, ct * S:(ct + 1) * S], wh[:, k, cut], wl[:, k, cut], hhi[:, k, :], hlo[:, k, :], k == 0, k == KT - 1)
                    if kind == "ki":
                        for t in range(TT):
                            tok = slice(t * P, (t + 1) * P)
                            for k in range(KT):
                                last = three(bank[:, S + t * H_I:S + (t + 1) * H_I], hhi[:, k, tok], hlo[:, k, tok],
                                             wh[:, k, P:P + H_I], wl[:, k, P:P + H_I], k == 0, k == KT - 1)
                last.then_inc(proj_done, 1)

            def sum_squares(l, n):
                j = NORMED.index(n)
                pe.wait_ge(sq_ready, nth(l, len(NORMED), j + 1))
                if j >= 1:
                    pe.wait_ge(rqk_ready, nth(l, len(NORMED), j))
                pe.matmul(SSB[:, :].rearrange("p (a s) -> p a s", a=2), heads1[:, :], sqr[:, :, :], start=True, stop=True).then_inc(ssq_done, 1)

            def pair(l, job, products):
                j = PAIRS.index(job)
                if job in LATE:
                    pe.wait_ge(proj_act, nth(l, NC - len(NORMED), copied(NC - 2)))
                elif j >= 1:
                    if PAIRS[j - 1][:3] == "rel":
                        pe.wait_ge(rel_read, nth(l, 3, j))
                    else:
                        pe.wait_ge(pair_read, nth(l, 8, PAIR_READS.index(PAIRS[j - 1]) + 1))
                for n, (head, lhsT, rhs, w) in enumerate(products):
                    bank = in_pair(job)[head % 2]
                    last = pe.matmul(bank[:, (n // 2) * w:(n // 2 + 1) * w], lhsT, rhs, start=True, stop=True)
                last.then_inc(pair_done, 1)

            def head_rows(h):
                return slice((h % 2) * HD, (h % 2 + 1) * HD)

            def relevance(l, j):
                if j == 0:
                    pe.wait_ge(proj_act, nth(l, NC - len(NORMED), 3))
                t = 0 if j == 0 else 1
                tok = slice(t * P, (t + 1) * P)
                heads = {0: range(8), 1: range(4), 2: range(4, 8)}[j]
                w = P * (t + 1)
                pair(l, f"rel{j}", [(h, qk1[head_rows(h), h // 2, tok], kiT[head_rows(h), 0:w], w) for h in heads])

            def attend(l, job):
                t = int(job[-1])
                tok = slice(t * P, (t + 1) * P)
                w = width(job)
                if t == 0:
                    pe.wait_ge(proj_dve, nth(l, len(NORMED), {"C00": 2, "C10": 4, "A0": 6}[job]))
                if job[0] == "A":
                    q, k = qk1[:, 0:2, :], qk1[:, 2:4, :]
                else:
                    g = int(job[1])
                    q, k = qcT[:, 2 * g:2 * g + 2, :], kcT[:, 2 * g:2 * g + 2, :]
                pair(l, job, [(h, q[head_rows(h), h // 2, tok], k[head_rows(h), h // 2, 0:w], w) for h in range(GRP)])

            def stick(l, st):
                if st == 0:
                    pe.wait_ge(proj_act, nth(l, NC - len(NORMED), copied(7)))
                pair(l, f"Z{st}", [(h, kbT[head_rows(h), h // 2, st * P:(st + 1) * P], qbT[head_rows(h), h // 2, st * P:S], S - st * P)
                                   for h in range(GRP)])

            def cumulate(l):
                pe.wait_ge(log1m_ready, nth(l, 2, 2))
                pe.wait_ge(rqk_ready, nth(l, len(NORMED), len(NORMED)))
                pe.wait_ge(pT_ready, nth(l, len(TRS), TRS.index(("C01", 1)) + 1))
                pe.wait_ge(o_read, nth(l, len(PVS), PVS.index("C01") + 1))
                for j in range(2):
                    hs = slice(2 * j, 2 * j + 2)
                    both = CUM[j][:, :].rearrange("p (h s) -> p h s", h=2)
                    pe.matmul(both, upper[:, :], e0[:, hs, :], start=True, stop=False)
                    pe.matmul(both[:, :, P:S], ones[:, :], e1[:, hs, :], start=False, stop=True).then_inc(cum_done, 1)
                pe.matmul(CUM[2][:, :].rearrange("p (h s) -> p h s", h=4), upper[:, :], e1, start=True, stop=True).then_inc(cum_done, 1)

            def turn_probs(l, job, *blocks):
                j = SOFT.index(job)
                lg = logits_of(job)
                pe.wait_ge(exps_ready, nth(l, len(SOFT), j + 1))
                if job == "C10":
                    pe.wait_ge(zc_ready, nth(l, 3, 2))
                for b in blocks:
                    n = TRS.index((job, b))
                    if n >= 1:
                        pe.wait_ge(pT_ready, nth(l, len(TRS), n))
                    for h in range(GRP):
                        last = pe.transpose(TRB[:, h * P:(h + 1) * P], lg[:, h, b * P:(b + 1) * P], ident[:, :])
                    last.then_inc(tr_done, 1)

            def values(l, job):
                t = int(job[-1])
                n = PVS.index(job)
                if job[0] == "B":
                    pe.wait_ge(a_ready, nth(l, 3, 3))
                    off = H_A * HD
                    probs = lambda b, h: z1[:, h, :] if b == 1 else z0[:, h, t * P:(t + 1) * P]
                else:
                    pe.wait_ge(pT_ready, nth(l, len(TRS), TRS.index((job, t)) + 1))
                    off = 0 if job[0] == "A" else (H_A + H_B) * HD + int(job[1]) * GRP * HD
                    probs = lambda b, h: pT[:, b, h, :]
                if job == "C10":
                    pe.wait_ge(zc_ready, nth(l, 3, 3))
                if n >= 1:
                    pe.wait_ge(o_read, nth(l, len(PVS), n))
                for h in range(GRP):
                    for b in range(t + 1):
                        last = pe.matmul(PVB[:, h * HD:(h + 1) * HD], probs(b, h), vs[:, b, off + h * HD:off + (h + 1) * HD],
                                         start=(b == 0), stop=(b == t))
                last.then_inc(pv_done, 1)

            for n in range(AHEAD // 2):
                sum_ada(n + 1, [0, 1], SB_).then_inc(modc_done, 1)
            with pe.Fori(0, L) as l:
                turn_h(l, 0)
                ffn(l, 0)
                pe.wait_ge(gate_ready, nth(l, 2 * NB, 2))
                turn_h(l, 1)
                wait_h(l, 1)
                for n in range(NC):
                    project(l, n)
                    if n == 0:
                        spread_gate(l, 1)
                    if n in (3, 4, 5):
                        relevance(l, n - 3)
                    if n - 1 in NORMED:
                        sum_squares(l, n - 1)
                    if n in (6, 7):
                        attend(l, f"C0{n - 6}")
                    if n in (8, 9):
                        stick(l, n - 8)
                    if n == 9:
                        turn_probs(l, "C00", 0)
                    if n == 10:
                        values(l, "C00")
                        turn_probs(l, "C01", 0)
                    if n == 11:
                        attend(l, "C10")
                        turn_probs(l, "C01", 1)
                    if n == 12:
                        values(l, "C01")
                        attend(l, "C11")
                    if n == 13:
                        attend(l, "A0")
                        cumulate(l)
                attend(l, "A1")
                turn_probs(l, "C10", 0)
                values(l, "C10")
                turn_probs(l, "C11", 0, 1)
                values(l, "C11")
                values(l, "B0")
                values(l, "B1")
                turn_probs(l, "A0", 0)
                values(l, "A0")
                turn_probs(l, "A1", 0, 1)
                values(l, "A1")
                turn_h(l, 3)
                wait_h(l, 3)
                for n, (k0, nk) in enumerate(OUT_CHUNKS):
                    slot = n % NSLOT
                    pe.wait_ge(split_done[slot], turn(l, U_OUT + n // NSLOT) + 2)
                    for k in range(nk):
                        kt = k0 + k
                        for t in range(TT):
                            tok = slice(t * P, (t + 1) * P)
                            for half in range(2):
                                w = slice(k * D + half * HALF, k * D + (half + 1) * HALF)
                                last = three(DB[2 * t + half][:, :], hhi[:, kt, tok], hlo[:, kt, tok], whi[slot][:, w], wlo[slot][:, w],
                                             kt == 0, kt == KT - 1)
                    last.then_inc(out_done, 1)
                for n in range(MID):
                    last = sum_ada(nth(l, ACC_L, AHEAD // 2 + NF + n + 1), [n], PVB, n * CT)
                last.then_inc(modc_done, 1)
                turn_h(l, 2)
                ffn(l, 1)


_INS = ['x', 'c', 'w_ada', 'b_ada', 'norm_ffn1', 'w_gate1', 'w_up1', 'w_down1', 'norm_mix', 'w_in', 'qn_a', 'kn_a',
        'qn_c', 'kn_c', 'g_out', 'w_out', 'norm_ffn2', 'w_gate2', 'w_up2', 'w_down2']


def kernel(**inputs):
    import numpy as _np
    import concourse.bacc as _bacc
    from concourse import mybir as _mybir
    from concourse.bass_utils import run_bass_kernel_spmd as _run

    nc = _bacc.Bacc("TRN2", target_bir_lowering=False, num_devices=1)
    arrays, args = {}, []
    for name in _INS:
        a = _np.ascontiguousarray(inputs[name])
        arrays[f"in_{name}_dram"] = a
        args.append(nc.dram_tensor(f"in_{name}_dram", a.shape, _mybir.dt.from_np(a.dtype), kind="ExternalInput").ap())
    shape = inputs["x"].shape
    args.append(nc.dram_tensor("out_0_dram", shape, _mybir.dt.float32, kind="ExternalOutput").ap())
    build(nc, *args)
    r = _run(nc, [arrays], core_ids=[0])
    return r.results[0]["out_0_dram"]
```

```python
from contextlib import ExitStack

import numpy as np

import concourse.bass as bass
from concourse import mybir

F32 = mybir.dt.float32
F32R = mybir.dt.float32r
BF16 = mybir.dt.bfloat16
I32 = mybir.dt.int32
ALU = mybir.AluOpType
ACT = mybir.ActivationFunctionType
AX_X = mybir.AxisListType.X

P = 128
HD = 64
H_A, H_B, H_C, H_I = 4, 4, 8, 8
DILATIONS = ((128, 1), (512, 4), (2048, 16))
EPS = 1e-6
NEG = -1e30
TAKEN = -3e38
CW = 256
NSLOT = 3
N_MOD = 9
GRP = 4


def slopes():
    n = H_A + H_C
    every = np.exp2(np.float32(-8.0) * np.arange(1, n + 1, dtype=np.float32) / np.float32(n))
    return [float(s) for i, s in enumerate(every) if i % 3 == 2], [float(s) for i, s in enumerate(every) if i % 3 != 2]


def build(nc, x, c, w_ada, b_ada, norm_ffn1, w_gate1, w_up1, w_down1, norm_mix, w_in, qn_a, kn_a, qn_c, kn_c,
          g_out, w_out, norm_ffn2, w_gate2, w_up2, w_down2, out):
    _, S, D = x.shape
    L = w_in.shape[0]
    FF = w_gate1.shape[2]
    KT = D // P
    TT = S // P
    NF = FF // CW
    FT = FF // P
    HALF = 512
    TOPK = min(256, S // 4)
    assert D == 1024 and S == 256 and FF % CW == 0 and TT == 2 and TOPK % 8 == 0

    sizes = [H_A * HD] * 3 + [H_I * HD, HD, H_I] + [H_B * HD] * 3 + [H_C * HD] * 3
    at = dict(zip(("qa", "ka", "va", "qi", "ki", "wi", "qb", "kb", "vb", "qc", "kc", "vc"), np.cumsum([0] + sizes[:-1]).tolist()))
    CHUNKS = [("qi", 0), ("qi", 1), ("ki", 0), ("kc", 0), ("qc", 0), ("vc", 0), ("kb", 0), ("qb", 0),
              ("kc", 1), ("qc", 1), ("ka", 0), ("qa", 0), ("vb", 0), ("vc", 1), ("va", 0)]
    NC = len(CHUNKS)
    NORMED = [n for n, (k, _) in enumerate(CHUNKS) if k in ("ka", "qa", "kc", "qc")]
    GAIN = {"qa": 0, "ka": 1, "qc": 2, "kc": 3}
    OUT_CHUNKS = [(0, 1), (1, 1), (2, 1), (3, 1), (4, 2), (6, 2)]
    U_FFN = (0, NF + NC // NSLOT + len(OUT_CHUNKS) // NSLOT)
    U_IN = NF
    U_OUT = NF + NC // NSLOT
    U_LAYER = U_FFN[1] + NF
    ADA_L = N_MOD * D // CW
    AHEAD = 2 * D // CW
    MID = ADA_L - 3 * NF
    CT = CW // P
    assert MID == 3 and KT * N_MOD == ADA_L * CT
    ADA_PRE = 2
    ADA_TURNS = (NF + 2 + NF, NF + 1)

    wide = lambda w: w.rearrange("l (k p) n -> p (l k) n", p=P)
    v_gate, v_up, v_down = map(wide, (w_gate1, w_up1, w_down1))
    v_gate2, v_up2, v_down2 = map(wide, (w_gate2, w_up2, w_down2))
    v_in, v_out, v_ada = map(wide, (w_in, w_out, w_ada))
    x_v = x.rearrange("b (t p) d -> p (b t) d", p=P)
    out_v = out.rearrange("b (t p) d -> p (b t) d", p=P)

    ctx = ExitStack()
    with ctx:
        def sb(name, shape, dt=F32):
            return ctx.enter_context(nc.sbuf_tensor(name, shape, dt))

        def sem(name):
            return ctx.enter_context(nc.semaphore(name))

        raws = sb("raw", [P, NSLOT, 8 * CW])
        raw = [raws[:, k, :] for k in range(NSLOT)]
        whi = [sb(f"whi{k}", [P, 8 * CW], F32R) for k in range(NSLOT)]
        wlo = [sb(f"wlo{k}", [P, 8 * CW], F32R) for k in range(NSLOT)]
        ada = sb("ada", [P, 2, KT, CW])
        xs = sb("xs", [P, TT, D])
        xn = sb("xn", [P, TT, D])
        hTf = sb("hTf", [P, KT, S])
        hhi = sb("hhi", [P, KT, S], F32R)
        hlo = sb("hlo", [P, KT, S], F32R)
        gate = sb("gate", [P, D])
        heads = sb("heads", [P, 16, S])
        sqr = sb("sqr", [P, 2, S])
        rqk = sb("rqk", [P, 2, S])
        selb = sb("selb", [P, P + S])
        kiT = sb("kiT", [P, S])
        vs = sb("vs", [P, TT, D])
        wi = sb("wi", [P, TT, H_I])
        aliA = sb("aliA", [P, H_A, S])
        aliC = sb("aliC", [P, H_C, S])
        causal = sb("causal", [P, S])
        strictT = sb("strictT", [P, S], BF16)
        ident = sb("ident", [P, P])
        ones = sb("ones", [P, P])
        heads1 = sb("heads1", [P, P])
        upper = sb("upper", [P, P])
        zero16 = sb("zero16", [P, P], BF16)
        LG = [sb(f"LG{k}", [P, 4 * S]) for k in range(2)]
        pT = sb("pT", [P, 3, GRP, P])
        eb = sb("eb", [P, GRP * (S + P)])
        guhi = sb("guhi", [P, 2 * S], F32R)
        gulo = sb("gulo", [P, 2 * S], F32R)
        top8 = sb("top8", [P, 8])
        cT = sb("cT", [P, KT])
        acc = sb("acc", [P, 2, CW])
        modc = sb("modc", [P, (N_MOD + 2) * KT])
        biasL = sb("biasL", [P, N_MOD, KT])
        cols = sb("cols", [P, L, KT, 13])
        colL = sb("colL", [P, KT, 13])
        qkg = sb("qkg", [P, L, 4])
        qkgL = sb("qkgL", [P, 4])
        modA = sb("modA", [P, KT])
        modB = sb("modB", [P, KT])
        ss = sb("ss", [P, TT, 4])
        var = sb("var", [P, TT, 4])
        rs = sb("rs", [P, TT, 4])
        tn = sb("tn", [P, TT, 4])
        mx = sb("mx", [P, 6, GRP])
        sm = sb("sm", [P, 6, GRP])
        rsm = sb("rsm", [P, 6, GRP])
        eps = sb("eps", [P, 1])
        qk1, qcT, kcT, qbT, kbT = (heads[:, a:b, :] for a, b in ((0, 4), (4, 8), (8, 12), (12, 14), (14, 16)))
        pre_ada = [ada[:, :, :, :]] + [raws[:, 0:2, :].rearrange("p a (k n) -> p a k n", k=KT), heads[:, :, :].rearrange("p (a k) n -> p a k n", a=2)] + [ada[:, :, :, :]]
        pre_acc = [acc[:, 0:2, :]] + [w.rearrange("p (a n) -> p a n", a=2) for w in (gate[:, 0:HALF], gate[:, HALF:D], eb[:, 0:HALF])]
        rows = vs[0:N_MOD + 4, :, :]
        score = acc
        silu = eb[:, 0:2 * S]
        guf = eb[:, 2 * S:4 * S]
        zf = hTf[:, :, :].rearrange("p k s -> p (k s)")
        z0 = zf[:, 0:GRP * S].rearrange("p (h s) -> p h s", h=GRP)
        z1 = zf[:, GRP * S:GRP * (S + P)].rearrange("p (h s) -> p h s", h=GRP)
        e0 = eb[:, 0:GRP * S].rearrange("p (h s) -> p h s", h=GRP)
        e1 = eb[:, GRP * S:GRP * (S + P)].rearrange("p (h s) -> p h s", h=GRP)
        disti = hTf[:, 0, :].bitcast(I32)
        dm4 = hTf[:, 1, :].bitcast(I32)
        dm16 = hTf[:, 2, :].bitcast(I32)
        strict_i = hTf[:, 3, :].bitcast(I32)
        upper_i = hTf[:, 4, 0:P].bitcast(I32)
        ident_i = hTf[:, 5, 0:P].bitcast(I32)
        distf = xn[:, 0, 0:S]
        ge0 = xn[:, 0, S:2 * S]
        tmpf = xn[:, 0, 2 * S:3 * S]
        maskC = xn[:, 0, 3 * S:4 * S]

        PS = [ctx.enter_context(nc.psum_tensor(f"bank{i}", [P, HALF], F32)) for i in range(8)]
        DB = PS[0:4]
        GB, UB0, UB1, SB_ = PS[4], PS[5], PS[6], PS[7]
        PROJ = [PS[0], PS[1], PS[7]]
        EVEN, ODD, SSB, TRB, PVB = PS[3], PS[4], PS[2], PS[5], PS[6]
        CUM = (PS[2], PS[0], PS[1])

        raw_full = [sem(f"raw_full{k}") for k in range(NSLOT)]
        hi_full = [sem(f"hi_full{k}") for k in range(NSLOT)]
        split_done = [sem(f"split_done{k}") for k in range(NSLOT)]
        ada_full = [sem(f"ada_full{k}") for k in range(2)]
        pre_full = [sem(f"pre_full{k}") for k in range(2)]
        ada_used = [sem(f"ada_used{k}") for k in range(2)]
        acc_ready = sem("acc_ready")
        modc_done = sem("modc_done")
        diag_ready = sem("diag_ready")
        gate_done = sem("gate_done")
        x_in = sem("x_in")
        rows_in = sem("rows_in")
        gains_in = sem("gains_in")
        c_in = sem("c_in")
        iotas = sem("iotas")
        tables = sem("tables")
        silu_c = sem("silu_c")
        cols_done = sem("cols_done")
        x_out = sem("x_out")
        rs_ready = sem("rs_ready")
        xn_ready = sem("xn_ready")
        tp_done = sem("tp_done")
        hTf_ready = sem("hTf_ready")
        mods_ready = sem("mods_ready")
        hhi_ready = sem("hhi_ready")
        h_ready = sem("h_ready")
        out_done = sem("out_done")
        gate_ready = sem("gate_ready")
        g_done = sem("g_done")
        silu_ready = sem("silu_ready")
        u_done = sem("u_done")
        gu_ready = sem("gu_ready")
        guhi_ready = sem("guhi_ready")
        gulo_ready = sem("gulo_ready")
        d_done = sem("d_done")
        x_ready = sem("x_ready")
        proj_done = sem("proj_done")
        proj_act = sem("proj_act")
        proj_dve = sem("proj_dve")
        sq_ready = sem("sq_ready")
        ssq_done = sem("ssq_done")
        rqk_ready = sem("rqk_ready")
        pair_done = sem("pair_done")
        rel_read = sem("rel_read")
        rel_used = sem("rel_used")
        pair_read = sem("pair_read")
        logits_ready = sem("logits_ready")
        exps_ready = sem("exps_ready")
        tr_done = sem("tr_done")
        pT_ready = sem("pT_ready")
        pv_done = sem("pv_done")
        o_read = sem("o_read")
        ln_ready = sem("ln_ready")
        log1m_ready = sem("log1m_ready")
        cum_done = sem("cum_done")
        zc_ready = sem("zc_ready")
        a_ready = sem("a_ready")

        block = ctx.enter_context(nc.Block())

        PAIRS = ["rel0", "rel1", "rel2", "C00", "C01", "Z0", "Z1", "C10", "C11", "A0", "A1"]
        SOFT = ["C00", "C01", "C10", "C11", "A0", "A1"]
        TRS = [(s, b) for s in SOFT for b in range(int(s[-1]) + 1)]
        PVS = ["C00", "C01", "C10", "B0", "C11", "B1", "A0", "A1"]
        PAIR_READS = PAIRS[3:]
        TPB = ((PS[4], PS[5]), (PS[6], PS[7]))
        GATES = ((PS[4], PS[5]), (PS[7], PS[2]), (PS[4], PS[5]))
        LATE = ("A1",)
        LOGITS = [LG[0], LG[1], zf[:, GRP * (S + P):KT * S], LG[0], LG[1], eb]
        TR_BANK = [PS[7] if tr in (("C11", 1), ("A1", 0)) else TRB for tr in TRS]
        PV_BANK = [PS[2] if job in ("B0", "B1", "A1") else PVB for job in PVS]

        def last_in_bank(banks, n):
            return max([m + 1 for m in range(n) if banks[m] is banks[n]], default=0)


        def in_pair(job):
            return (PS[0], PS[1]) if job in LATE else (EVEN, ODD)

        def width(job):
            return P * (int(job[-1]) + 1)

        def logits_of(job):
            return LOGITS[SOFT.index(job)][:, 0:GRP * width(job)].rearrange("p (h s) -> p h s", h=GRP)

        def chunk_cols(w, n=CW):
            return w[:, :].rearrange("p (k n) -> p k n", k=8)[:, :, 0:n]

        def at_cols(start, n):
            return slice(start, start + n) if isinstance(start, int) else bass.ds(start, n)

        def turn(l, n):
            return l * U_LAYER + n

        def copied(n):
            return sum(m not in NORMED for m in range(n + 1))

        def nth(l, per_layer, n):
            return l * per_layer + n

        def ada_turn(l, slot, n):
            return ADA_PRE + l * ADA_TURNS[slot] + n

        MODC_PRE = 1
        MODC_L = NF + 2 + NF
        ACC_L = NF + MID + NF

        NB = 3
        GROUPS = [H_A * HD, H_B * HD, H_C * HD]
        NN = 4 * TT
        NORM_AT = {0: 0, 1: 1, 3: 2, 2: 3}

        @block.sync
        def _(sp):
            sp.dma_start(cT[:, :], c.rearrange("b (k p) -> p (b k)", p=P), allow_slow_non_contiguous=True).then_inc(c_in, 16)
            sp.dma_start(rows[0:N_MOD, :, :], b_ada.rearrange("l (m d) -> m l d", d=D)).then_inc(rows_in, 16)
            for n, g in enumerate((norm_ffn1, norm_mix, norm_ffn2, g_out)):
                sp.dma_start(rows[N_MOD + n:N_MOD + n + 1, :, :], g.rearrange("(a l) d -> a l d", a=1)).then_inc(rows_in, 16)
            for n, g in enumerate((qn_a, kn_a, qn_c, kn_c)):
                for half in range(2):
                    sp.dma_start(qkg[half * HD:half * HD + HD, :, n], g.rearrange("l p -> p l"),
                                 allow_slow_non_contiguous=True).then_inc(gains_in, 16)
            sp.wait_ge(ada_full[0], 16)
            sp.dma_start(xs[:, :, :], x_v).then_inc(x_in, 16)

            def fill(slot, use, dst, src, waited=False):
                if not waited:
                    sp.wait_ge(split_done[slot], use + 1)
                sp.dma_start(dst, src).then_inc(raw_full[slot], 16)

            def gate_up(use, k0, f0, wg, wu):
                fill(0, use, chunk_cols(raw[0]), wg[:, at_cols(k0, KT), at_cols(f0, CW)])
                fill(1, use, chunk_cols(raw[1]), wu[:, at_cols(k0, KT), at_cols(f0, CW)])

            def down(use, r0, wd):
                fill(2, use, raw[2][:, :].rearrange("p (k n) -> p k n", k=2), wd[:, bass.ds(r0, 2), :])

            def ffn(l, base, wg, wu, wd):
                with sp.Fori(0, NF - 1) as i:
                    use, k0, f0, r0 = (sp.snap(v) for v in (turn(l, base) + i, l * KT, i * CW + CW, l * FT + i * 2))
                    down(use, r0, wd)
                    gate_up(sp.snap(use + 1), k0, f0, wg, wu)
                down(turn(l, base) + (NF - 1), sp.snap(l * FT + (NF - 1) * 2), wd)

            sp.wait_ge(acc_ready, 2)
            gate_up(0, 0, 0, v_gate, v_up)
            QA = CHUNKS.index(("qa", 0))
            with sp.Fori(0, L) as l:
                ffn(l, U_FFN[0], v_gate, v_up, v_down)
                k_in = sp.snap(l * KT)
                for n, (kind, part) in enumerate(CHUNKS):
                    w = HD + H_I if kind == "ki" else CW
                    col = at[kind] + part * CW
                    if n == QA - 1:
                        for m in (QA - 1, QA):
                            sp.wait_ge(split_done[m % NSLOT], turn(l, U_IN + m // NSLOT) + 1)
                    fill(n % NSLOT, turn(l, U_IN + n // NSLOT), chunk_cols(raw[n % NSLOT], w),
                         v_in[:, bass.ds(k_in, KT), col:col + w], waited=n in (QA - 1, QA))
                for n, (k0, nk) in enumerate(OUT_CHUNKS):
                    fill(n % NSLOT, turn(l, U_OUT + n // NSLOT),
                         raw[n % NSLOT][:, 0:nk * D].rearrange("p (k n) -> p k n", k=nk), v_out[:, bass.ds(l * KT + k0, nk), :])
                gate_up(turn(l, U_FFN[1]), k_in, 0, v_gate2, v_up2)
                ffn(l, U_FFN[1], v_gate2, v_up2, v_down2)
                gate_up(turn(l, U_LAYER), sp.snap((l + 1) % L * KT), 0, v_gate, v_up)
            for t in range(TT):
                sp.wait_ge(x_ready, NB * TT * L + t + 1)
                sp.dma_start(out_v[:, t, :], xs[:, t, :]).then_inc(x_out, 16)
            sp.wait_ge(x_out, 16 * TT)

        @block.gpsimd
        def _(pool):
            def fill(slot, turn_, row, col):
                pool.wait_ge(ada_used[slot], turn_)
                pool.dma_start(ada[:, slot, :, :], v_ada[:, row, col]).then_inc(ada_full[slot], 16)

            pool.iota(disti, pattern=[[-1, S]], base=P, channel_multiplier=1).then_inc(iotas, 1)
            pool.iota(strict_i, pattern=[[1, S]], base=0, channel_multiplier=-1).then_inc(iotas, 1)
            pool.iota(upper_i, pattern=[[-1, P]], base=0, channel_multiplier=1).then_inc(iotas, 1)

            for m in range(AHEAD):
                pair, k = m // 2, m % 2
                col = slice(m * CW, (m + 1) * CW)
                if pair in (1, 2):
                    pool.dma_start(pre_ada[pair][:, k, :, :], v_ada[:, 0:KT, col]).then_inc(pre_full[pair - 1], 16)
                else:
                    fill(k, 1 + pair // 3, slice(0, KT), col)
            with pool.Fori(0, L) as l:
                rows_l = pool.snap(l * KT)
                with pool.Fori(0, NF) as i:
                    for k in range(2):
                        fill(k, ada_turn(l, k, i + 1), bass.ds(rows_l, KT), bass.ds(i * (2 * CW) + (AHEAD + k) * CW, CW))
                for n in range(MID):
                    m = AHEAD + 2 * NF + n
                    fill(n % 2, ada_turn(l, n % 2, NF + n // 2 + 1), bass.ds(rows_l, KT), slice(m * CW, (m + 1) * CW))
                with pool.Fori(0, NF - AHEAD) as i:
                    fill(0, ada_turn(l, 0, NF + 2 + i + 1), bass.ds(rows_l, KT), bass.ds(i * CW + (ADA_L - (NF - AHEAD)) * CW, CW))
                rows_n = pool.snap((l + 1) % L * KT)
                with pool.Fori(0, AHEAD) as i:
                    fill(0, ada_turn(l, 0, NF + 2 + NF - AHEAD + i + 1), bass.ds(rows_n, KT), bass.ds(i * CW, CW))

        @block.scalar
        def _(act):
            act.wait_ge(c_in, 16)
            act.activation(cT[:, :], cT[:, :], ACT.Silu).then_inc(silu_c, 1)

            def split_hi(slot, use, pieces=None):
                act.wait_ge(raw_full[slot], (use + 1) * 16)
                if pieces is None:
                    pieces = [(whi[slot][:, :], raw[slot][:, :])]
                for dst, src in pieces:
                    last = act.activation(dst, src, ACT.Copy)
                last.then_inc(hi_full[slot], 1)

            def root(t, counts):
                act.drain()
                for a, b in ((0, 1),) if len(counts) == 1 else ((0, 2), (2, 3)):
                    act.activation(rs[:, t, a:b], ss[:, t, a:b], ACT.Ln, scale=1.0 / counts[a], bias=eps[:, :])
                act.drain()
                act.activation(rs[:, t, 0:len(counts)], rs[:, t, 0:len(counts)], ACT.Exp, scale=-0.5).then_inc(rs_ready, 1)

            def boundary(l, n, x_done):
                for t in range(TT):
                    act.wait_ge(x_ready, x_done + t + 1)
                    act.activation(xn[:, t, :], xs[:, t, :], ACT.Square, accum_out=ss[:, t, 0:1])
                    root(t, [D])
                if n in (0, 2):
                    act.preload_act_table(ACT.Silu)
                high_of_h(l, n)

            def copy_gate(l, n):
                act.wait_ge(gate_done, nth(l, NB, n + 1))
                for half in range(2):
                    last = act.activation(gate[:, half * HALF:(half + 1) * HALF], GATES[n][half][:, :], ACT.Copy,
                                          scale=1.0 if n == 1 else 0.5)
                last.then_inc(gate_ready, 1)

            def high_of_h(l, n):
                if n < 3:
                    act.wait_ge(mods_ready, nth(l, NB, n + 1))
                for t in range(TT):
                    act.wait_ge(tp_done, nth(l, 4 * 2 * TT, (NORM_AT[n] * TT + t) * 2 + 1))
                    for k in range(4):
                        dst, src = hTf[:, k, t * P:(t + 1) * P], TPB[t][0][:, k * P:(k + 1) * P]
                        if n < 3:
                            act.activation(dst, src, ACT.Identity, scale=modA[:, k:k + 1], bias=modB[:, k:k + 1])
                        else:
                            act.activation(dst, src, ACT.Identity, scale=colL[:, k, 12:13])
                    act.drain()
                    act.wait_ge(hTf_ready, nth(l, NN, NORM_AT[n] * TT + t + 1))
                    act.activation(hhi[:, :, t * P:(t + 1) * P], hTf[:, :, t * P:(t + 1) * P], ACT.Copy).then_inc(hhi_ready, 1)

            def ffn_step(l, which, i, ahead, after):
                base = turn(l, U_FFN[which])
                n = nth(l, 2 * NF, which * NF) + i
                act.wait_ge(g_done, n + 1)
                act.activation(silu, GB[:, :], ACT.Silu).then_inc(silu_ready, 1)
                split_hi(2, base + i)
                for ft in range(2):
                    act.wait_ge(gu_ready, n * 2 + ft + 1)
                    act.activation(guhi[:, ft * S:(ft + 1) * S], guf[:, ft * S:(ft + 1) * S], ACT.Copy).then_inc(guhi_ready, 1)
                    if ft == 0 or ahead:
                        split_hi(ft, after + i if ahead else after)
                if not ahead:
                    copy_gate(l, 2 * which)
                    split_hi(1, after)

            def ffn(l, which, after):
                with act.Fori(0, NF - 1) as i:
                    ffn_step(l, which, i, True, turn(l, U_FFN[which] + 1))
                ffn_step(l, which, NF - 1, False, turn(l, after))
                act.preload_act_table_set("natural_log_exp_and_others")

            def mix_split(l, n):
                slot = n % NSLOT
                pieces = None
                if CHUNKS[n][0] == "ki":
                    r = chunk_cols(raw[slot])
                    w = chunk_cols(whi[slot])
                    pieces = [(w[:, :, 0:HD], r[:, :, 0:HD]), (w[:, :, HD:2 * HD], r[:, :, 0:HD]),
                              (w[:, :, P:P + H_I], r[:, :, HD:HD + H_I])]
                split_hi(slot, turn(l, U_IN + n // NSLOT), pieces)

            def evacuate(l, n):
                kind, part = CHUNKS[n]
                bank = PROJ[n % 3]
                act.wait_ge(proj_done, nth(l, NC, n + 1))
                if n in NORMED:
                    act.activation(sqr[:, :, :], bank[:, :].rearrange("p (a s) -> p a s", a=2), ACT.Square).then_inc(sq_ready, 1)
                    return
                both = bank[:, :].rearrange("p (a s) -> p a s", a=2)
                if kind == "qi":
                    last = act.activation(qk1[:, 2 * part:2 * part + 2, :], both, ACT.Copy)
                elif kind == "ki":
                    act.activation(kiT[:, :], bank[:, 0:S], ACT.Copy)
                    last = act.activation(wi[:, :, :], bank[:, S:S + TT * H_I].rearrange("p (t h) -> p t h", t=TT), ACT.Copy)
                elif kind in ("qb", "kb"):
                    last = act.activation((qbT if kind == "qb" else kbT)[:, :, :], both, ACT.Copy)
                else:
                    off = {"va": 0, "vb": H_A * HD, "vc": (H_A + H_B) * HD}[kind] + part * CW
                    last = act.activation(vs[:, :, off:off + CW], both, ACT.Copy)
                last.then_inc(proj_act, 1)

            def inv_rms(l, n):
                j = NORMED.index(n)
                act.wait_ge(ssq_done, nth(l, len(NORMED), j + 1))
                if j >= 1:
                    act.wait_ge(proj_dve, nth(l, len(NORMED), j))
                act.activation(rqk[:, :, :], SSB[:, :].rearrange("p (a s) -> p a s", a=2), ACT.Ln, scale=1.0 / HD, bias=eps[:, :])
                act.drain()
                act.activation(rqk[:, :, :], rqk[:, :, :], ACT.Exp, scale=-0.5).then_inc(rqk_ready, 1)

            def rel_relu(l, j):
                act.wait_ge(pair_done, nth(l, len(PAIRS), j + 1))
                if j >= 2:
                    act.wait_ge(rel_used, nth(l, 3, j - 1))
                for odd in range(2):
                    last = act.activation(LG[j % 2][:, odd * HALF:(odd + 1) * HALF], (EVEN, ODD)[odd][:, :], ACT.Relu)
                last.then_inc(rel_read, 1)

            def exps(l, job):
                j = SOFT.index(job)
                act.wait_ge(logits_ready, nth(l, len(SOFT), j + 1))
                lg = logits_of(job)
                for h in range(GRP):
                    last = act.activation(lg[:, h, :], lg[:, h, :], ACT.Exp, bias=mx[:, j, h:h + 1], accum_out=sm[:, j, h:h + 1])
                last.then_inc(exps_ready, 1)

            def copy_pT(l, job, *blocks):
                for b in blocks:
                    n = TRS.index((job, b))
                    act.wait_ge(tr_done, nth(l, len(TRS), n + 1))
                    act.activation(pT[:, n % 3, :, :], TR_BANK[n][:, :].rearrange("p (h t) -> p h t", h=GRP), ACT.Copy).then_inc(pT_ready, 1)

            def softplus_log(l, st):
                z, e = ((z0, e0), (z1, e1))[st]
                act.wait_ge(pair_read, nth(l, 8, PAIR_READS.index(f"Z{st}") + 1))
                act.activation(e, z, ACT.Abs)
                act.drain()
                act.activation(e, e, ACT.Exp, scale=-1.0)
                act.drain()
                act.activation(e, e, ACT.Ln, bias=1.0).then_inc(ln_ready, 1)

            def stick_exps(l):
                for j in range(3):
                    act.wait_ge(zc_ready, nth(l, 3, j + 1))
                    part = z1 if j == 2 else z0[:, 2 * j:2 * j + 2, :]
                    act.activation(part, part, ACT.Exp).then_inc(a_ready, 1)

            act.wait_ge(tables, 2)
            act.wait_ge(x_in, 16)
            act.preload_act_table_set("natural_log_exp_and_others")
            for k in range(2):
                split_hi(k, 0)
            with act.Fori(0, L) as l:
                boundary(l, 0, nth(l, NB * TT, 0))
                ffn(l, 0, U_IN)
                boundary(l, 1, nth(l, NB * TT, TT))
                for n in range(NC + 1):
                    if n >= 2 and n - 2 in NORMED:
                        inv_rms(l, n - 2)
                    if n >= 1:
                        evacuate(l, n - 1)
                    if n + 2 < NC:
                        mix_split(l, n + 2)
                    if n in (4, 5, 6):
                        rel_relu(l, n - 4)
                    if n == 1:
                        copy_gate(l, 1)
                    if n == 8:
                        exps(l, "C00")
                    if n == 9:
                        exps(l, "C01")
                    if n == 10:
                        copy_pT(l, "C00", 0)
                        softplus_log(l, 0)
                    if n == 11:
                        copy_pT(l, "C01", 0)
                        softplus_log(l, 1)
                    if n == 12:
                        copy_pT(l, "C01", 1)
                    if n == 13:
                        exps(l, "C10")
                    if n == 14:
                        copy_pT(l, "C10", 0)
                        exps(l, "C11")
                exps(l, "A0")
                stick_exps(l)
                copy_pT(l, "C11", 0, 1)
                split_hi(0, turn(l, U_OUT), [(whi[0][:, 0:D], raw[0][:, 0:D])])
                exps(l, "A1")
                copy_pT(l, "A0", 0)
                copy_pT(l, "A1", 0, 1)
                for k in range(1, NSLOT):
                    split_hi(k, turn(l, U_OUT), [(whi[k][:, 0:D], raw[k][:, 0:D])])
                for t in range(TT):
                    act.wait_ge(o_read, nth(l, len(PVS), len(PVS) - 1 + t))
                    for g, (a, b) in enumerate(((0, 256), (256, 512), (512, 1024))):
                        act.activation((sqr[:, 0, :], sqr[:, 1, :], rqk[:, :, :].rearrange("p a s -> p (a s)"))[g], xn[:, t, a:b], ACT.Square, accum_out=ss[:, t, g:g + 1])
                    root(t, GROUPS)
                high_of_h(l, 3)
                for n in range(NSLOT, len(OUT_CHUNKS)):
                    k = n % NSLOT
                    nk = OUT_CHUNKS[n][1]
                    act.wait_ge(out_done, nth(l, len(OUT_CHUNKS) - 1, n - NSLOT + 1))
                    split_hi(k, turn(l, U_OUT + 1), [(whi[k][:, 0:nk * D], raw[k][:, 0:nk * D])])
                for k in range(2):
                    act.wait_ge(out_done, nth(l, len(OUT_CHUNKS) - 1, NSLOT + k + 1))
                    split_hi(k, turn(l, U_FFN[1]))
                boundary(l, 2, nth(l, NB * TT, 2 * TT))
                ffn(l, 1, U_LAYER)

        @block.vector
        def _(dve):
            for k in range(NSLOT):
                dve.sem_inc(split_done[k], 1)
            for k in range(2):
                dve.sem_inc(ada_used[k], 1)
            dve.memset(zero16[:, :], 0.0)
            dve.memset(ones[:, :], 1.0)
            dve.memset(heads1[:, :], 0.0)
            dve.memset(eps[:, :], EPS)
            dve.drain()
            for k in range(2):
                dve.memset(heads1[k * HD:(k + 1) * HD, k * HD:(k + 1) * HD], 1.0)
            dve.wait_ge(iotas, 3)
            dve.tensor_scalar(ident[:, :], upper_i, 0.0, None, ALU.is_equal)
            dve.tensor_scalar(upper[:, :], upper_i, 0.0, None, ALU.is_ge).then_inc(tables, 1)
            dve.tensor_scalar(strictT[:, :], strict_i, 0.0, NEG, ALU.is_le, ALU.mult)
            dve.tensor_scalar(dm4, disti, DILATIONS[1][1] - 1, None, ALU.bitwise_and)
            dve.tensor_scalar(dm16, disti, DILATIONS[2][1] - 1, None, ALU.bitwise_and)
            dve.tensor_copy(distf, disti)
            dve.drain()
            dve.tensor_scalar(ge0, distf, 0.0, None, ALU.is_ge)
            dve.tensor_scalar(causal[:, :], distf, 0.0, NEG, ALU.is_lt, ALU.mult)
            dve.tensor_scalar(tmpf, dm4, 0.0, None, ALU.is_equal)
            dve.tensor_scalar(maskC, dm16, 0.0, None, ALU.is_equal)
            dve.drain()
            dve.tensor_tensor(tmpf, tmpf, maskC, ALU.add)
            dve.drain()
            dve.scalar_tensor_tensor(tmpf, distf, float(DILATIONS[0][0]), tmpf, ALU.is_le, ALU.add)
            dve.drain()
            dve.tensor_tensor(tmpf, tmpf, ge0, ALU.mult)
            dve.drain()
            dve.tensor_scalar(maskC, tmpf, 0.0, NEG, ALU.is_equal, ALU.mult)
            for m in (2, 3):
                dve.drain()
                dve.tensor_scalar(ge0, tmpf, float(m), float(np.log(m)), ALU.is_equal, ALU.mult)
                dve.drain()
                dve.tensor_tensor(maskC, maskC, ge0, ALU.add)
            dve.drain()
            s_a, s_c = slopes()
            for h in range(H_A):
                dve.scalar_tensor_tensor(aliA[:, h, :], distf, -s_a[h], causal[:, :], ALU.mult, ALU.add)
            for h in range(H_C):
                dve.scalar_tensor_tensor(aliC[:, h, :], distf, -s_c[h], maskC, ALU.mult, ALU.add)
            def late_tables():
                dve.wait_ge(cols_done, 1)
                dve.tensor_copy(cols[:, :, :, :], PS[0][:, 0:L * KT * 13].rearrange("p (l k m) -> p l k m", l=L, k=KT))
                dve.wait_ge(x_in, 16)
                dve.sem_inc(x_ready, TT)
                dve.wait_ge(gains_in, 8 * 16)
                dve.drain().then_inc(tables, 1)

            def weigh_rows(sums, chunks):
                for k in range(KT):
                    if k == 0:
                        dve.tensor_scalar(sums, chunks[:, :, k, :], cT[:, 0:1], None, ALU.mult)
                    else:
                        last = dve.scalar_tensor_tensor(sums, chunks[:, :, k, :], cT[:, k:k + 1], sums, ALU.mult, ALU.add)
                    if k < KT - 1:
                        dve.drain()
                last.then_inc(acc_ready, 1)

            def weigh_ada(turns, slots, sums):
                for slot, n in zip(slots, turns):
                    dve.wait_ge(ada_full[slot], n * 16)
                weigh_rows(sums, ada[:, slots[0]:slots[-1] + 1, :, :])
                for slot in slots:
                    dve.drain().then_inc(ada_used[slot], 1)

            def weigh_mid(l, m):
                weigh_ada([ada_turn(l, m % 2, NF + m // 2 + 1)], [m % 2], acc[:, m % 2:m % 2 + 1, :])

            def read_modc(done, dst, bank):
                dve.wait_ge(modc_done, done)
                dve.tensor_copy(dst, bank)

            def diagonal(n):
                off = (3 * n + 2) * KT
                dve.drain()
                dve.tensor_tensor(modc[:, off:off + KT], modc[:, off:off + KT], biasL[:, 3 * n + 2, :], ALU.add)
                dve.drain()
                for k in range(KT):
                    last = dve.tensor_scalar(gate[:, k * P:(k + 1) * P], ident[:, :], modc[:, off + k:off + k + 1], None, ALU.mult)
                last.then_inc(diag_ready, 1)

            def split_lo(slot, use, pieces=None):
                dve.wait_ge(hi_full[slot], use + 1)
                if pieces is None:
                    pieces = [(wlo[slot][:, :], raw[slot][:, :], whi[slot][:, :])]
                for dst, src, hi in pieces:
                    last = dve.tensor_tensor(dst, src, hi.bitcast(F32), ALU.subtract)
                last.then_inc(split_done[slot], 1)

            def refine(l, n, t, groups, counts):
                dve.wait_ge(rs_ready, nth(l, NN, NORM_AT[n] * TT + t + 1))
                for a, b in ((0, 1),) if groups == 1 else ((0, 2), (2, 3)):
                    dve.tensor_scalar(var[:, t, a:b], ss[:, t, a:b], 1.0 / counts[a], EPS, ALU.mult, ALU.add)
                dve.tensor_tensor(tn[:, t, 0:groups], rs[:, t, 0:groups], rs[:, t, 0:groups], ALU.mult)
                dve.drain()
                dve.tensor_tensor(tn[:, t, 0:groups], tn[:, t, 0:groups], var[:, t, 0:groups], ALU.mult)
                dve.drain()
                dve.tensor_scalar(tn[:, t, 0:groups], tn[:, t, 0:groups], -0.5, 1.5, ALU.mult, ALU.add)
                dve.drain()
                src = xs if n < 3 else xn
                for cut, g in (((0, HALF), 0), ((HALF, D), 0)) if n < 3 else (((0, 256), 0), ((256, 512), 1), ((512, D), 2)):
                    last = dve.tensor_scalar(xn[:, t, cut[0]:cut[1]], src[:, t, cut[0]:cut[1]], rs[:, t, g:g + 1], tn[:, t, g:g + 1], ALU.mult, ALU.mult)
                    if cut[1] in (HALF, D):
                        last.then_inc(xn_ready, 1)

            def transposed(l, n, gain, shift):
                for t in range(TT):
                    dve.wait_ge(tp_done, nth(l, 4 * 2 * TT, (NORM_AT[n] * TT + t) * 2 + 2))
                    bank = TPB[t][1]
                    for k in range(4):
                        last = dve.tensor_scalar(hTf[:, 4 + k, t * P:(t + 1) * P], bank[:, k * P:(k + 1) * P], gain[:, 4 + k:5 + k],
                                                 None if shift is None else shift[:, 4 + k:5 + k], ALU.mult,
                                                 **({} if shift is None else {"op1": ALU.add}))
                    last.then_inc(hTf_ready, 1)
                for t in range(TT):
                    dve.wait_ge(hhi_ready, nth(l, NN, NORM_AT[n] * TT + t + 1))
                    tok = slice(t * P, (t + 1) * P)
                    dve.tensor_tensor(hlo[:, :, tok], hTf[:, :, tok], hhi[:, :, tok].bitcast(F32), ALU.subtract).then_inc(h_ready, 1)

            def modulation(l, n):
                off = 3 * n * KT
                dve.drain()
                dve.tensor_tensor(modB[:, :], modc[:, off:off + KT], biasL[:, 3 * n, :], ALU.add)
                dve.tensor_tensor(modA[:, :], modc[:, off + KT:off + 2 * KT], biasL[:, 3 * n + 1, :], ALU.add)
                dve.drain()
                dve.scalar_tensor_tensor(modA[:, :], modA[:, :], 1.0, colL[:, :, N_MOD + n], ALU.add, ALU.mult).then_inc(mods_ready, 1)

            def boundary(l, n):
                for t in range(TT):
                    refine(l, n, t, 1, [D])
                transposed(l, n, modA, modB)

            def residual(l, n):
                dve.wait_ge(gate_ready, nth(l, NB, n + 1))
                for t in range(TT):
                    dve.wait_ge(d_done, nth(l, NB * TT, n * TT + t + 1))
                    for half in range(2):
                        cut = slice(half * HALF, (half + 1) * HALF)
                        dve.tensor_tensor(xn[:, t, cut], DB[2 * t + half][:, :], gate[:, cut], ALU.mult)
                    dve.drain()
                    dve.tensor_tensor(xs[:, t, :], xs[:, t, :], xn[:, t, :], ALU.add).then_inc(x_ready, 1)

            def ffn_step(l, which, i, ahead, after):
                base = turn(l, U_FFN[which])
                n = nth(l, 2 * NF, which * NF) + i
                if not ahead:
                    diagonal(2 * which)
                if which == 0:
                    weigh_ada([ada_turn(l, k, i + 1) for k in range(2)], [0, 1], acc[:, 0:2, :])
                else:
                    weigh_ada([ada_turn(l, 0, NF + 2 + i + 1)], [0], acc[:, 0:1, :])
                dve.wait_ge(hi_full[2], base + i + 1)
                dve.tensor_tensor(wlo[2][:, 0:D], raw[2][:, 0:D], whi[2][:, 0:D].bitcast(F32), ALU.subtract)
                dve.wait_ge(silu_ready, n + 1)
                for ft in range(2):
                    cut = slice(ft * S, (ft + 1) * S)
                    dve.wait_ge(u_done, n * 2 + ft + 1)
                    dve.tensor_tensor(guf[:, cut], silu[:, cut], (UB0, UB1)[ft][:, 0:S], ALU.mult).then_inc(gu_ready, 1)
                    dve.wait_ge(guhi_ready, n * 2 + ft + 1)
                    dve.tensor_tensor(gulo[:, cut], guf[:, cut], guhi[:, cut].bitcast(F32), ALU.subtract).then_inc(gulo_ready, 1)
                    if ft == 0:
                        dve.tensor_tensor(wlo[2][:, D:2 * D], raw[2][:, D:2 * D], whi[2][:, D:2 * D].bitcast(F32), ALU.subtract).then_inc(split_done[2], 1)
                if which == 0:
                    read_modc(MODC_PRE + nth(l, MODC_L, 1) + i, modc[:, at_cols(AHEAD * CT + i * (2 * CT), 2 * CT)], SB_[:, 0:2 * CT])
                else:
                    read_modc(MODC_PRE + nth(l, MODC_L, NF + 3) + i, modc[:, at_cols((AHEAD + 2 * NF + MID) * CT + i * CT, CT)], SB_[:, 0:CT])
                if not ahead and which == 0:
                    modulation(l, 1)
                split_lo(0, after + i if ahead else after)
                if ahead:
                    split_lo(1, after + i)

            def ffn(l, which, after):
                with dve.Fori(0, NF - 1) as i:
                    ffn_step(l, which, i, True, turn(l, U_FFN[which] + 1))
                ffn_step(l, which, NF - 1, False, turn(l, after))
                residual(l, 2 * which)

            def mix_split(l, n):
                slot = n % NSLOT
                pieces = None
                if CHUNKS[n][0] == "ki":
                    r, w, v = chunk_cols(raw[slot]), chunk_cols(whi[slot]), chunk_cols(wlo[slot])
                    pieces = [(v[:, :, 0:HD], r[:, :, 0:HD], w[:, :, 0:HD]), (v[:, :, HD:2 * HD], r[:, :, 0:HD], w[:, :, HD:2 * HD]),
                              (v[:, :, P:P + H_I], r[:, :, HD:HD + H_I], w[:, :, P:P + H_I])]
                split_lo(slot, turn(l, U_IN + n // NSLOT), pieces)

            def head_norm(l, n):
                kind, part = CHUNKS[n]
                j = NORMED.index(n)
                dve.wait_ge(rqk_ready, nth(l, len(NORMED), j + 1))
                dst = {"qa": qk1[:, 0:2, :], "ka": qk1[:, 2:4, :], "qc": qcT[:, 2 * part:2 * part + 2, :],
                       "kc": kcT[:, 2 * part:2 * part + 2, :]}[kind]
                both = lambda a: a.rearrange("p (a s) -> p a s", a=2)
                dve.scalar_tensor_tensor(dst, both(PROJ[n % 3][:, :]), qkgL[:, GAIN[kind]:GAIN[kind] + 1], rqk[:, :, :],
                                         ALU.mult, ALU.mult).then_inc(proj_dve, 1)

            def weigh(l, j):
                dve.wait_ge(rel_read, nth(l, 3, j + 1))
                t = 0 if j == 0 else 1
                w = P * (t + 1)
                n_heads = 8 if j == 0 else 4
                sc = score[:, t, 0:w]
                for h in range(n_heads):
                    head = h + (4 if j == 2 else 0)
                    src = LG[j % 2][:, (h % 2) * HALF + (h // 2) * w:(h % 2) * HALF + (h // 2 + 1) * w]
                    if head == 0:
                        last = dve.tensor_scalar(sc, src, wi[:, t, 0:1], None, ALU.mult)
                    else:
                        last = dve.scalar_tensor_tensor(sc, src, wi[:, t, head:head + 1], sc, ALU.mult, ALU.add)
                    if h == n_heads - 1:
                        last.then_inc(rel_used, 1)
                    dve.drain()
                if j != 1:
                    dve.scalar_tensor_tensor(sc, sc, HD ** -0.5 * H_I ** -0.5, causal[:, S - w:S], ALU.mult, ALU.add)
                    dve.drain()

            def take_top(t, rounds):
                sc = score[:, t, 0:P * (t + 1)]
                for _ in range(rounds):
                    dve.max(top8[:, :], sc)
                    dve.drain()
                    dve.match_replace(sc, top8[:, :], sc, TAKEN)
                    dve.drain()

            def select(t):
                w = P * (t + 1)
                dve.tensor_scalar(selb[:, t * P:t * P + w], score[:, t, 0:w], TAKEN, NEG, ALU.not_equal, ALU.mult)
                dve.drain()

            def logits(l, job):
                j = SOFT.index(job)
                w = width(job)
                lg = logits_of(job)
                even, odd = in_pair(job)
                bias = aliA if job[0] == "A" else aliC[:, GRP * int(job[1]):GRP * (int(job[1]) + 1), :]
                dve.wait_ge(pair_done, nth(l, len(PAIRS), PAIRS.index(job) + 1))
                if j >= 3:
                    dve.wait_ge(tr_done, nth(l, len(TRS), TRS.index((SOFT[j - 3], int(SOFT[j - 3][-1]))) + 1))
                for odd_, bank in enumerate((even, odd)):
                    last = dve.scalar_tensor_tensor(lg[:, odd_::2, :], bank[:, 0:2 * w].rearrange("p (h s) -> p h s", h=2), HD ** -0.5,
                                                    bias[:, odd_::2, S - w:S], ALU.mult, ALU.add)
                last.then_inc(pair_read, 1)
                dve.drain()
                if job[0] == "A":
                    t = int(job[-1])
                    dve.tensor_tensor(lg, lg, selb[:, t * P:t * P + w].unsqueeze(1).to_broadcast([P, GRP, w]), ALU.add)
                    dve.drain()
                dve.tensor_reduce(mx[:, j, :], lg, AX_X, ALU.max)
                dve.drain()
                dve.tensor_scalar(mx[:, j, :], mx[:, j, :], -1.0, None, ALU.mult).then_inc(logits_ready, 1)

            def read_out(l, job):
                t = int(job[-1])
                off = {"A": 0, "B": H_A * HD}.get(job[0], (H_A + H_B) * HD + (int(job[1]) * GRP * HD if job[0] == "C" else 0))
                if job[0] != "B":
                    j = SOFT.index(job)
                    dve.wait_ge(exps_ready, nth(l, len(SOFT), j + 1))
                    dve.reciprocal(rsm[:, j, :], sm[:, j, :])
                    dve.drain()
                dve.wait_ge(pv_done, nth(l, len(PVS), PVS.index(job) + 1))
                dst = xn[:, t, off:off + GRP * HD]
                src = PV_BANK[PVS.index(job)][:, 0:GRP * HD]
                if job[0] == "B":
                    dve.tensor_copy(dst, src).then_inc(o_read, 1)
                else:
                    dve.tensor_tensor(dst.rearrange("p (h d) -> p h d", h=GRP), src.rearrange("p (h d) -> p h d", h=GRP),
                                      rsm[:, j, :].unsqueeze(2).to_broadcast([P, GRP, HD]), ALU.mult).then_inc(o_read, 1)

            def stick_logits(l, st):
                z = (z0, z1)[st]
                w = S - st * P
                dve.wait_ge(pair_done, nth(l, len(PAIRS), PAIRS.index(f"Z{st}") + 1))
                for odd_, bank in enumerate((EVEN, ODD)):
                    last = dve.scalar_tensor_tensor(z[:, odd_::2, :], bank[:, 0:2 * w].rearrange("p (h s) -> p h s", h=2), HD ** -0.5,
                                                    strictT[:, 0:w].unsqueeze(1).to_broadcast([P, 2, w]), ALU.mult, ALU.add)
                last.then_inc(pair_read, 1)

            def softplus(l, st):
                z, e = ((z0, e0), (z1, e1))[st]
                dve.wait_ge(ln_ready, nth(l, 2, st + 1))
                dve.scalar_tensor_tensor(e, z, 0.0, e, ALU.max, ALU.add).then_inc(log1m_ready, 1)

            def minus_cum(l):
                for j in range(3):
                    part = z1 if j == 2 else z0[:, 2 * j:2 * j + 2, :]
                    dve.wait_ge(cum_done, nth(l, 3, j + 1))
                    dve.tensor_tensor(part, part, CUM[j][:, :].rearrange("p (h s) -> p h s", h=4 if j == 2 else 2), ALU.subtract).then_inc(zc_ready, 1)

            dve.wait_ge(silu_c, 1)
            for n in range(AHEAD // 2):
                if n in (1, 2):
                    dve.wait_ge(pre_full[n - 1], 2 * 16)
                    weigh_rows(pre_acc[n], pre_ada[n])
                else:
                    weigh_ada([1 + n // 3] * 2, [0, 1], pre_acc[n])
            late_tables()
            split_lo(0, 0)
            read_modc(1, modc[:, N_MOD * KT:(N_MOD + 2) * KT], SB_[:, 0:2 * KT])
            dve.drain()
            with dve.Fori(0, L) as l:
                dve.tensor_copy(colL[:, :, :], cols[:, bass.ds(l, 1), :, :].rearrange("p a k m -> p (a k) m"))
                dve.tensor_copy(modc[:, 0:2 * KT], modc[:, N_MOD * KT:(N_MOD + 2) * KT])
                dve.tensor_copy(biasL[:, :, :], cols[:, bass.ds(l, 1), :, 0:N_MOD].rearrange("p a k m -> p m (a k)"))
                dve.tensor_copy(qkgL[:, :], qkg[:, bass.ds(l, 1), :].rearrange("p a k -> p (a k)"))
                modulation(l, 0)
                boundary(l, 0)
                split_lo(1, turn(l, U_FFN[0]))
                ffn(l, 0, U_IN)
                boundary(l, 1)
                mix_split(l, 1)
                for n in range(NC + 1):
                    if n >= 2 and n - 2 in NORMED:
                        head_norm(l, n - 2)
                    if n + 2 < NC:
                        mix_split(l, n + 2)
                    if n == 0:
                        diagonal(1)
                    if n in (1, 2):
                        weigh_mid(l, n - 1)
                    if n == 4:
                        off = (AHEAD + 2 * NF) * CT
                        read_modc(MODC_PRE + nth(l, MODC_L, NF + 1), modc[:, off:off + 2 * CT], PVB[:, 0:2 * CT])
                    if n == 4:
                        weigh(l, 0)
                        take_top(0, TOPK // 16)
                    if n == 5:
                        weigh(l, 1)
                        take_top(0, TOPK // 16)
                        select(0)
                    if n == 6:
                        weigh(l, 2)
                        take_top(1, TOPK // 64)
                    if n == 7:
                        logits(l, "C00")
                        take_top(1, TOPK // 32)
                    if n == 8:
                        logits(l, "C01")
                    if n == 9:
                        stick_logits(l, 0)
                        take_top(1, TOPK // 32)
                    if n == 10:
                        stick_logits(l, 1)
                        take_top(1, TOPK // 64)
                    if n == 11:
                        read_out(l, "C00")
                        softplus(l, 0)
                        take_top(1, TOPK // 32)
                        select(1)
                    if n == 12:
                        softplus(l, 1)
                        logits(l, "C10")
                    if n == 13:
                        read_out(l, "C01")
                        logits(l, "C11")
                    if n == 14:
                        logits(l, "A0")
                        minus_cum(l)
                        read_out(l, "C10")
                logits(l, "A1")
                read_out(l, "B0")
                read_out(l, "C11")
                read_out(l, "B1")
                first_out = lambda k: split_lo(k, turn(l, U_OUT), [(wlo[k][:, 0:D], raw[k][:, 0:D], whi[k][:, 0:D])])
                first_out(0)
                read_out(l, "A0")
                read_out(l, "A1")
                for t in range(TT):
                    refine(l, 3, t, 3, GROUPS)
                first_out(1)
                transposed(l, 3, colL[:, :, 12], None)
                first_out(2)
                for n in range(NSLOT, len(OUT_CHUNKS)):
                    k = n % NSLOT
                    nk = OUT_CHUNKS[n][1]
                    split_lo(k, turn(l, U_OUT + 1), [(wlo[k][:, 0:nk * D], raw[k][:, 0:nk * D], whi[k][:, 0:nk * D])])
                    if n == NSLOT:
                        weigh_mid(l, 2)
                split_lo(0, turn(l, U_FFN[1]))
                off = (AHEAD + 2 * NF + 2) * CT
                read_modc(MODC_PRE + nth(l, MODC_L, NF + 2), modc[:, off:off + CT], PVB[:, 0:CT])
                modulation(l, 2)
                residual(l, 1)
                boundary(l, 2)
                split_lo(1, turn(l, U_FFN[1]))
                ffn(l, 1, U_LAYER)

        @block.tensor
        def _(pe):
            pe.wait_ge(tables, 1)
            pe.wait_ge(rows_in, 5 * 16)
            for l in range(L):
                for k in range(KT):
                    o = (l * KT + k) * 13
                    last = pe.transpose(PS[0][:, o:o + 13], rows[:, l, k * P:(k + 1) * P], ident[0:13, 0:13])
            last.then_inc(cols_done, 1)

            def three(ps, l_hi, l_lo, r_hi, r_lo, first, last):
                pe.matmul(ps, l_hi, r_hi, start=first, stop=False)
                pe.matmul(ps, l_hi, r_lo, start=False, stop=False)
                return pe.matmul(ps, l_lo, r_hi, start=False, stop=last)

            def sum_ada(ready, slots, bank, at_=0, sums=acc):
                pe.wait_ge(acc_ready, ready)
                for slot in slots:
                    for j in range(CT):
                        last = pe.matmul(bank[:, at_:at_ + 1], sums[:, slot, j * P:(j + 1) * P], ones[:, 0:1], start=True, stop=True)
                        at_ += 1
                return last

            def spread_gate(l, n, *halves):
                pe.wait_ge(diag_ready, nth(l, NB, n + 1))
                for half in halves:
                    last = pe.matmul(GATES[n][half][:, :], ones[:, :], gate[:, half * HALF:(half + 1) * HALF], start=True, stop=True)
                if halves[-1] == 1:
                    last.then_inc(gate_done, 1)

            def turn_h(l, n):
                for t in range(TT):
                    for half in range(2):
                        pe.wait_ge(xn_ready, nth(l, 2 * NN, (NORM_AT[n] * TT + t) * 2 + half + 1))
                        for k in range(4):
                            kk = half * 4 + k
                            last = pe.transpose(TPB[t][half][:, k * P:(k + 1) * P], xn[:, t, kk * P:(kk + 1) * P], ident[:, :])
                        last.then_inc(tp_done, 1)

            def wait_high(l, n, t=TT - 1):
                pe.wait_ge(hhi_ready, nth(l, NN, NORM_AT[n] * TT + t + 1))

            def wait_low(l, n, t=TT - 1):
                pe.wait_ge(h_ready, nth(l, NN, NORM_AT[n] * TT + t + 1))

            def by_high(l, n, ps, wh, wl):
                for k in range(KT):
                    pe.matmul(ps, wh[:, k, :], hhi[:, k, :], start=k == 0, stop=False)
                    pe.matmul(ps, wl[:, k, :], hhi[:, k, :], start=False, stop=False)
                wait_low(l, n)
                for k in range(KT):
                    last = pe.matmul(ps, wh[:, k, :], hlo[:, k, :], start=False, stop=k == KT - 1)
                return last

            def ffn_step(l, which, i, is_last):
                use = turn(l, U_FFN[which]) + i
                n = nth(l, 2 * NF, which * NF) + i
                pe.wait_ge(split_done[0], use + 2)
                wh, wl = chunk_cols(whi[0]), chunk_cols(wlo[0])
                for ft in range(2):
                    last = by_high(l, 2 * which, GB[:, ft * S:(ft + 1) * S], wh[:, :, ft * P:(ft + 1) * P], wl[:, :, ft * P:(ft + 1) * P])
                last.then_inc(g_done, 1)
                pe.wait_ge(split_done[1], use + 2)
                wh, wl = chunk_cols(whi[1]), chunk_cols(wlo[1])
                for ft in range(2):
                    for k in range(KT):
                        last = three((UB0, UB1)[ft][:, 0:S], wh[:, k, ft * P:(ft + 1) * P], wl[:, k, ft * P:(ft + 1) * P],
                                     hhi[:, k, :], hlo[:, k, :], k == 0, k == KT - 1)
                    last.then_inc(u_done, 1)
                if which == 0:
                    sum_ada(nth(l, ACC_L, AHEAD // 2 + 1) + i, [0, 1], SB_).then_inc(modc_done, 1)
                else:
                    sum_ada(nth(l, ACC_L, AHEAD // 2 + NF + MID + 1) + i, [0], SB_).then_inc(modc_done, 1)
                if is_last:
                    pe.wait_ge(silu_ready, n + 1)
                    spread_gate(l, 2 * which, 0)

                def down(ft, t, close):
                    tok = slice(ft * S + t * P, ft * S + (t + 1) * P)
                    for half in range(2):
                        w = slice(ft * D + half * HALF, ft * D + (half + 1) * HALF)
                        last = three(DB[2 * t + half][:, :], guhi[:, tok], gulo[:, tok], whi[2][:, w], wlo[2][:, w], False, close)
                    return last

                pe.wait_ge(gulo_ready, n * 2 + 1)
                if is_last:
                    spread_gate(l, 2 * which, 1)
                    down(0, 0, False)
                else:
                    for t in range(TT):
                        down(0, t, False)
                pe.wait_ge(split_done[2], use + 2)
                pe.wait_ge(gulo_ready, n * 2 + 2)
                if is_last:
                    down(1, 0, True).then_inc(d_done, 1)
                    down(0, 1, False)
                    down(1, 1, True).then_inc(d_done, 1)
                else:
                    for t in range(TT):
                        down(1, t, False)

            def ffn(l, which):
                for b in range(4):
                    if b == 3:
                        wait_high(l, 2 * which)
                    pe.matmul(DB[b][:, :], zero16[:, :], zero16[:, :].unsqueeze(1).to_broadcast([P, HALF // P, P]), start=True, stop=False)
                with pe.Fori(0, NF - 1) as i:
                    ffn_step(l, which, i, False)
                ffn_step(l, which, NF - 1, True)

            def project(l, n):
                kind, part = CHUNKS[n]
                slot = n % NSLOT
                bank = PROJ[n % 3]
                pe.wait_ge(split_done[slot], turn(l, U_IN + n // NSLOT) + 2)
                if n >= 3:
                    if n - 3 in NORMED:
                        pe.wait_ge(proj_dve, nth(l, len(NORMED), NORMED.index(n - 3) + 1))
                    else:
                        pe.wait_ge(proj_act, nth(l, NC - len(NORMED), copied(n - 3)))
                elif n == 2:
                    pe.wait_ge(gate_ready, nth(l, NB, 2))
                wh, wl = chunk_cols(whi[slot]), chunk_cols(wlo[slot])
                if kind[0] == "v":
                    for t in range(TT):
                        tok = slice(t * P, (t + 1) * P)
                        for k in range(KT):
                            last = three(bank[:, t * CW:(t + 1) * CW], hhi[:, k, tok], hlo[:, k, tok], wh[:, k, :], wl[:, k, :], k == 0, k == KT - 1)
                else:
                    for ct in range(1 if kind == "ki" else 2):
                        if n == 0:
                            last = by_high(l, 1, bank[:, ct * S:(ct + 1) * S], wh[:, :, ct * P:(ct + 1) * P], wl[:, :, ct * P:(ct + 1) * P])
                            continue
                        for k in range(KT):
                            cut = slice(ct * P, (ct + 1) * P)
                            last = three(bank[:, ct * S:(ct + 1) * S], wh[:, k, cut], wl[:, k, cut], hhi[:, k, :], hlo[:, k, :], k == 0, k == KT - 1)
                    if kind == "ki":
                        for t in range(TT):
                            tok = slice(t * P, (t + 1) * P)
                            for k in range(KT):
                                last = three(bank[:, S + t * H_I:S + (t + 1) * H_I], hhi[:, k, tok], hlo[:, k, tok],
                                             wh[:, k, P:P + H_I], wl[:, k, P:P + H_I], k == 0, k == KT - 1)
                last.then_inc(proj_done, 1)

            def sum_squares(l, n):
                j = NORMED.index(n)
                pe.wait_ge(sq_ready, nth(l, len(NORMED), j + 1))
                if j >= 1:
                    pe.wait_ge(rqk_ready, nth(l, len(NORMED), j))
                pe.matmul(SSB[:, :].rearrange("p (a s) -> p a s", a=2), heads1[:, :], sqr[:, :, :], start=True, stop=True).then_inc(ssq_done, 1)

            def pair(l, job, products):
                j = PAIRS.index(job)
                if job in LATE:
                    pe.wait_ge(zc_ready, nth(l, 3, 3))
                elif j >= 1:
                    if PAIRS[j - 1][:3] == "rel":
                        pe.wait_ge(rel_read, nth(l, 3, j))
                    else:
                        pe.wait_ge(pair_read, nth(l, 8, PAIR_READS.index(PAIRS[j - 1]) + 1))
                for n, (head, lhsT, rhs, w) in enumerate(products):
                    bank = in_pair(job)[head % 2]
                    last = pe.matmul(bank[:, (n // 2) * w:(n // 2 + 1) * w], lhsT, rhs, start=True, stop=True)
                last.then_inc(pair_done, 1)

            def head_rows(h):
                return slice((h % 2) * HD, (h % 2 + 1) * HD)

            def relevance(l, j):
                if j == 0:
                    pe.wait_ge(proj_act, nth(l, NC - len(NORMED), 3))
                t = 0 if j == 0 else 1
                tok = slice(t * P, (t + 1) * P)
                heads = {0: range(8), 1: range(4), 2: range(4, 8)}[j]
                w = P * (t + 1)
                pair(l, f"rel{j}", [(h, qk1[head_rows(h), h // 2, tok], kiT[head_rows(h), 0:w], w) for h in heads])

            def attend(l, job):
                t = int(job[-1])
                tok = slice(t * P, (t + 1) * P)
                w = width(job)
                if t == 0:
                    pe.wait_ge(proj_dve, nth(l, len(NORMED), {"C00": 2, "C10": 4, "A0": 6}[job]))
                if job[0] == "A":
                    q, k = qk1[:, 0:2, :], qk1[:, 2:4, :]
                else:
                    g = int(job[1])
                    q, k = qcT[:, 2 * g:2 * g + 2, :], kcT[:, 2 * g:2 * g + 2, :]
                pair(l, job, [(h, q[head_rows(h), h // 2, tok], k[head_rows(h), h // 2, 0:w], w) for h in range(GRP)])

            def stick(l, st):
                if st == 0:
                    pe.wait_ge(proj_act, nth(l, NC - len(NORMED), copied(7)))
                pair(l, f"Z{st}", [(h, kbT[head_rows(h), h // 2, st * P:(st + 1) * P], qbT[head_rows(h), h // 2, st * P:S], S - st * P)
                                   for h in range(GRP)])

            def cumulate(l):
                pe.wait_ge(log1m_ready, nth(l, 2, 2))
                pe.wait_ge(rqk_ready, nth(l, len(NORMED), len(NORMED)))
                pe.wait_ge(proj_act, nth(l, NC - len(NORMED), copied(NC - 2)))
                for j in range(2):
                    hs = slice(2 * j, 2 * j + 2)
                    both = CUM[j][:, :].rearrange("p (h s) -> p h s", h=2)
                    pe.matmul(both, upper[:, :], e0[:, hs, :], start=True, stop=False)
                    pe.matmul(both[:, :, P:S], ones[:, :], e1[:, hs, :], start=False, stop=True).then_inc(cum_done, 1)
                pe.matmul(CUM[2][:, :].rearrange("p (h s) -> p h s", h=4), upper[:, :], e1, start=True, stop=True).then_inc(cum_done, 1)

            def turn_probs(l, job, *blocks):
                j = SOFT.index(job)
                lg = logits_of(job)
                pe.wait_ge(exps_ready, nth(l, len(SOFT), j + 1))
                for b in blocks:
                    n = TRS.index((job, b))
                    if last_in_bank(TR_BANK, n):
                        pe.wait_ge(pT_ready, nth(l, len(TRS), last_in_bank(TR_BANK, n)))
                    elif n:
                        pe.wait_ge(proj_act, nth(l, NC - len(NORMED), NC - len(NORMED)))
                    for h in range(GRP):
                        last = pe.transpose(TR_BANK[n][:, h * P:(h + 1) * P], lg[:, h, b * P:(b + 1) * P], ident[:, :])
                    last.then_inc(tr_done, 1)

            def values(l, job):
                t = int(job[-1])
                n = PVS.index(job)
                if job[0] == "B":
                    pe.wait_ge(a_ready, nth(l, 3, 3))
                    off = H_A * HD
                    probs = lambda b, h: z1[:, h, :] if b == 1 else z0[:, h, t * P:(t + 1) * P]
                else:
                    pe.wait_ge(pT_ready, nth(l, len(TRS), TRS.index((job, t)) + 1))
                    off = 0 if job[0] == "A" else (H_A + H_B) * HD + int(job[1]) * GRP * HD
                    probs = lambda b, h: pT[:, TRS.index((job, b)) % 3, h, :]
                if last_in_bank(PV_BANK, n):
                    pe.wait_ge(o_read, nth(l, len(PVS), last_in_bank(PV_BANK, n)))
                for h in range(GRP):
                    for b in range(t + 1):
                        last = pe.matmul(PV_BANK[n][:, h * HD:(h + 1) * HD], probs(b, h), vs[:, b, off + h * HD:off + (h + 1) * HD],
                                         start=(b == 0), stop=(b == t))
                last.then_inc(pv_done, 1)

            for n in range(AHEAD // 2):
                last = sum_ada(n + 1, [0, 1], SB_, n * 2 * CT, pre_acc[n])
            last.then_inc(modc_done, 1)
            with pe.Fori(0, L) as l:
                turn_h(l, 0)
                ffn(l, 0)
                pe.wait_ge(gate_ready, nth(l, NB, 1))
                turn_h(l, 1)
                wait_high(l, 1)
                for n in range(NC):
                    project(l, n)
                    if n == 0:
                        spread_gate(l, 1, 0, 1)
                    if n == 3:
                        for m in range(2):
                            last = sum_ada(nth(l, ACC_L, AHEAD // 2 + NF + m + 1), [m], PVB, m * CT)
                        last.then_inc(modc_done, 1)
                    if n in (3, 4, 5):
                        relevance(l, n - 3)
                    if n - 1 in NORMED:
                        sum_squares(l, n - 1)
                    if n in (6, 7):
                        attend(l, f"C0{n - 6}")
                    if n in (8, 9):
                        stick(l, n - 8)
                    if n == 9:
                        turn_probs(l, "C00", 0)
                    if n == 10:
                        values(l, "C00")
                        turn_probs(l, "C01", 0)
                    if n == 11:
                        attend(l, "C10")
                        turn_probs(l, "C01", 1)
                    if n == 12:
                        values(l, "C01")
                        attend(l, "C11")
                    if n == 13:
                        turn_probs(l, "C10", 0)
                        attend(l, "A0")
                        cumulate(l)
                values(l, "C10")
                attend(l, "A1")
                turn_probs(l, "C11", 0, 1)
                values(l, "B0")
                values(l, "C11")
                turn_probs(l, "A0", 0)
                values(l, "B1")
                values(l, "A0")
                turn_probs(l, "A1", 0, 1)
                values(l, "A1")
                turn_h(l, 3)
                for n, (k0, nk) in enumerate(OUT_CHUNKS):
                    slot = n % NSLOT
                    if n == len(OUT_CHUNKS) - 1:
                        sum_ada(nth(l, ACC_L, AHEAD // 2 + NF + MID), [(MID - 1) % 2], PVB).then_inc(modc_done, 1)
                    pe.wait_ge(split_done[slot], turn(l, U_OUT + n // NSLOT) + 2)
                    if n == 0:
                        for low in (False, True):
                            for t in range(TT):
                                (wait_low if low else wait_high)(l, 3, t)
                                tok = slice(t * P, (t + 1) * P)
                                for half in range(2):
                                    w = slice(half * HALF, (half + 1) * HALF)
                                    if low:
                                        last = pe.matmul(DB[2 * t + half][:, :], hlo[:, 0, tok], whi[slot][:, w], start=False, stop=False)
                                    else:
                                        pe.matmul(DB[2 * t + half][:, :], hhi[:, 0, tok], whi[slot][:, w], start=True, stop=False)
                                        pe.matmul(DB[2 * t + half][:, :], hhi[:, 0, tok], wlo[slot][:, w], start=False, stop=False)
                        last.then_inc(out_done, 1)
                        continue
                    for t in range(TT):
                        for k in range(nk):
                            kt = k0 + k
                            tok = slice(t * P, (t + 1) * P)
                            for half in range(2):
                                w = slice(k * D + half * HALF, k * D + (half + 1) * HALF)
                                last = three(DB[2 * t + half][:, :], hhi[:, kt, tok], hlo[:, kt, tok], whi[slot][:, w], wlo[slot][:, w],
                                             False, kt == KT - 1)
                        if n == len(OUT_CHUNKS) - 1:
                            last.then_inc(d_done, 1)
                    if n < len(OUT_CHUNKS) - 1:
                        last.then_inc(out_done, 1)
                turn_h(l, 2)
                ffn(l, 1)


_INS = ['x', 'c', 'w_ada', 'b_ada', 'norm_ffn1', 'w_gate1', 'w_up1', 'w_down1', 'norm_mix', 'w_in', 'qn_a', 'kn_a',
        'qn_c', 'kn_c', 'g_out', 'w_out', 'norm_ffn2', 'w_gate2', 'w_up2', 'w_down2']


def kernel(**inputs):
    import numpy as _np
    import concourse.bacc as _bacc
    from concourse import mybir as _mybir
    from concourse.bass_utils import run_bass_kernel_spmd as _run

    nc = _bacc.Bacc("TRN2", target_bir_lowering=False, num_devices=1)
    arrays, args = {}, []
    for name in _INS:
        a = _np.ascontiguousarray(inputs[name])
        arrays[f"in_{name}_dram"] = a
        args.append(nc.dram_tensor(f"in_{name}_dram", a.shape, _mybir.dt.from_np(a.dtype), kind="ExternalInput").ap())
    shape = inputs["x"].shape
    args.append(nc.dram_tensor("out_0_dram", shape, _mybir.dt.float32, kind="ExternalOutput").ap())
    build(nc, *args)
    r = _run(nc, [arrays], core_ids=[0])
    return r.results[0]["out_0_dram"]
```
